# Optimizing a Trainium2 kernel written in Bass

```python
import jax, jax.numpy as jnp
from jax import lax
import numpy as np

D_MODEL = 1024
BATCH = 1
SEQ = 256
DEPTH = 1

POOL_WINDOWS = (2, 4, 8, 16)
POOL_WIDTH = D_MODEL // 2
POOL_GROUP = POOL_WIDTH // len(POOL_WINDOWS)
HEAD_DIM = 64
N_HEADS = (D_MODEL // 2) // HEAD_DIM
N_KV_HEADS = 2
ATTN_WIDTH = N_HEADS * HEAD_DIM
KV_WIDTH = N_KV_HEADS * HEAD_DIM
WINDOW = 128
BLOCK = 128
ROPE_THETA = 500000.0
ROT_DIM = HEAD_DIM // 4
MIX_WIDTH = POOL_WIDTH + ATTN_WIDTH
IN_WIDTH = POOL_WIDTH + ATTN_WIDTH + 2 * KV_WIDTH
D_FF = 2816
EPS = 1e-6
NEG_INF = -1e30


def rms_norm(x, g):
    xf = x.astype(jnp.float32)
    y = xf * lax.rsqrt(jnp.mean(xf * xf, axis=-1, keepdims=True) + EPS)
    return (y * g.astype(jnp.float32)).astype(x.dtype)

def swiglu(h, w_gu, w_down):
    gate, up = jnp.split(h @ w_gu, 2, axis=-1)
    return (jax.nn.silu(gate) * up) @ w_down

def pool_mix(u, w_pool, pool_scale):
    B, S, C = u.shape
    uf = u.astype(jnp.float32)
    cs = jnp.concatenate([jnp.zeros((B, 1, C), jnp.float32), jnp.cumsum(uf, axis=1)], axis=1)
    t = jnp.arange(S)
    outs = []
    for g, w in enumerate(POOL_WINDOWS):
        lo, hi = g * POOL_GROUP, (g + 1) * POOL_GROUP
        start = jnp.maximum(t + 1 - w, 0)
        cnt = (t + 1 - start).astype(jnp.float32)
        csg = cs[:, :, lo:hi]
        mean = (csg[:, 1:] - csg[:, start]) / cnt[None, :, None]
        outs.append(mean - uf[:, :, lo:hi])
    d = jnp.stack(outs, axis=2).astype(u.dtype)
    y = jnp.einsum('bsgc,gcd->bsgd', d, w_pool).reshape(B, S, POOL_WIDTH)
    return y * pool_scale

def apply_partial_rope(x, cos, sin):
    half = ROT_DIM // 2
    x1, x2 = x[..., :half], x[..., half:ROT_DIM]
    rot = jnp.concatenate([x1 * cos - x2 * sin, x2 * cos + x1 * sin], axis=-1)
    return jnp.concatenate([rot, x[..., ROT_DIM:]], axis=-1)

def swa_with_sinks(q, k, v, sinks):
    B, S = q.shape[0], q.shape[1]
    nb = S // BLOCK
    G = N_HEADS // N_KV_HEADS
    qb = q.reshape(B, nb, BLOCK, N_KV_HEADS, G, HEAD_DIM)
    pad = ((0, 0), (BLOCK, 0), (0, 0), (0, 0))
    kp = jnp.pad(k, pad).reshape(B, nb + 1, BLOCK, N_KV_HEADS, HEAD_DIM)
    vp = jnp.pad(v, pad).reshape(B, nb + 1, BLOCK, N_KV_HEADS, HEAD_DIM)
    kb = jnp.concatenate([kp[:, :-1], kp[:, 1:]], axis=2)
    vb = jnp.concatenate([vp[:, :-1], vp[:, 1:]], axis=2)
    s = jnp.einsum('bnqkgd,bnjkd->bnkgqj', qb, kb,
                   preferred_element_type=jnp.float32) * (HEAD_DIM ** -0.5)
    qi = jnp.arange(BLOCK)[:, None]
    kj = jnp.arange(2 * BLOCK)[None, :]
    diff = qi + BLOCK - kj
    band = (diff >= 0) & (diff < WINDOW)
    key_abs = jnp.arange(nb)[:, None] * BLOCK - BLOCK + kj
    valid = band[None] & (key_abs >= 0)[:, None, :]
    s = jnp.where(valid[None, :, None, None], s, NEG_INF)
    sink = jnp.broadcast_to(sinks.astype(jnp.float32).reshape(1, 1, N_KV_HEADS, G, 1, 1),
                            s.shape[:-1] + (1,))
    p = jax.nn.softmax(jnp.concatenate([s, sink], axis=-1), axis=-1)[..., :-1]
    o = jnp.einsum('bnkgqj,bnjkd->bnqkgd', p.astype(v.dtype), vb)
    return o.reshape(B, S, ATTN_WIDTH)

def token_mixer(h, cos, sin, w_in, w_pool, pool_scale, sinks, g_pool, g_attn, w_out):
    B, S, _ = h.shape
    z = h @ w_in
    u = z[..., :POOL_WIDTH]
    q = z[..., POOL_WIDTH:MIX_WIDTH].reshape(B, S, N_HEADS, HEAD_DIM)
    k = z[..., MIX_WIDTH:MIX_WIDTH + KV_WIDTH].reshape(B, S, N_KV_HEADS, HEAD_DIM)
    v = z[..., MIX_WIDTH + KV_WIDTH:].reshape(B, S, N_KV_HEADS, HEAD_DIM)
    pool_out = pool_mix(u, w_pool, pool_scale)
    q = apply_partial_rope(q, cos, sin)
    k = apply_partial_rope(k, cos, sin)
    attn_out = swa_with_sinks(q, k, v, sinks)
    y = jnp.concatenate([rms_norm(pool_out, g_pool), rms_norm(attn_out, g_attn)], axis=-1)
    return y @ w_out

def first_inputs(seed: int = 0) -> dict:
    key = jax.random.key(seed)
    ks = jax.random.split(key, 24)
    f32 = jnp.float32

    def w(k, shape, fan_in):
        return jax.random.normal(k, shape, f32) * fan_in ** -0.5

    def gain(k, n):
        return 1.0 + 0.05 * jax.random.normal(k, (DEPTH, n), f32)

    x = jax.random.normal(ks[0], (BATCH, SEQ, D_MODEL), f32)
    offset = jax.random.randint(ks[1], (BATCH, 1), 0, 4096, jnp.int32)
    positions = offset + jnp.arange(SEQ, dtype=jnp.int32)[None, :]
    return {
        "x": x,
        "positions": positions,
        "ffn1_pre": gain(ks[2], D_MODEL),
        "ffn1_w_gu": w(ks[3], (DEPTH, D_MODEL, 2 * D_FF), D_MODEL),
        "ffn1_w_down": w(ks[4], (DEPTH, D_FF, D_MODEL), D_FF),
        "ffn1_post": gain(ks[5], D_MODEL),
        "mix_pre": gain(ks[6], D_MODEL),
        "w_in": w(ks[7], (DEPTH, D_MODEL, IN_WIDTH), D_MODEL),
        "w_pool": w(ks[8], (DEPTH, len(POOL_WINDOWS), POOL_GROUP, POOL_GROUP), POOL_GROUP),
        "pool_scale": 0.5 + 0.05 * jax.random.normal(ks[9], (DEPTH, POOL_WIDTH), f32),
        "sinks": 0.5 * jax.random.normal(ks[10], (DEPTH, N_HEADS), f32),
        "g_pool": gain(ks[11], POOL_WIDTH),
        "g_attn": gain(ks[12], ATTN_WIDTH),
        "w_out": w(ks[13], (DEPTH, MIX_WIDTH, D_MODEL), MIX_WIDTH),
        "mix_post": gain(ks[14], D_MODEL),
        "ffn2_pre": gain(ks[15], D_MODEL),
        "ffn2_w_gu": w(ks[16], (DEPTH, D_MODEL, 2 * D_FF), D_MODEL),
        "ffn2_w_down": w(ks[17], (DEPTH, D_FF, D_MODEL), D_FF),
        "ffn2_post": gain(ks[18], D_MODEL),
    }

def first_block(x, positions, ffn1_pre, ffn1_w_gu, ffn1_w_down, ffn1_post,
              mix_pre, w_in, w_pool, pool_scale, sinks, g_pool, g_attn, w_out, mix_post,
              ffn2_pre, ffn2_w_gu, ffn2_w_down, ffn2_post):
    inv_freq = ROPE_THETA ** (-jnp.arange(0, ROT_DIM, 2, dtype=jnp.float32) / ROT_DIM)
    ang = positions.astype(jnp.float32)[..., None] * inv_freq
    cos = jnp.cos(ang)[:, :, None, :].astype(x.dtype)
    sin = jnp.sin(ang)[:, :, None, :].astype(x.dtype)
    for l in range(DEPTH):
        h = swiglu(rms_norm(x, ffn1_pre[l]), ffn1_w_gu[l], ffn1_w_down[l])
        x = x + 0.5 * rms_norm(h, ffn1_post[l])
        h = token_mixer(rms_norm(x, mix_pre[l]), cos, sin, w_in[l], w_pool[l], pool_scale[l],
                        sinks[l], g_pool[l], g_attn[l], w_out[l])
        x = x + rms_norm(h, mix_post[l])
        h = swiglu(rms_norm(x, ffn2_pre[l]), ffn2_w_gu[l], ffn2_w_down[l])
        x = x + 0.5 * rms_norm(h, ffn2_post[l])
    return x


CHUNK = 64
Q_BLOCK = 128
N_MEM = 256

SSD_HEADS = 16
SSD_HEAD_DIM = 64
SSD_D_INNER = SSD_HEADS * SSD_HEAD_DIM
SSD_GROUPS = 4
SSD_STATE = 128
SSD_CONV = 4
SSD_XBC = SSD_D_INNER + 2 * SSD_GROUPS * SSD_STATE

MLA_HEADS = 16
MLA_Q_RANK = 384
MLA_KV_RANK = 256
MLA_NOPE = 64
MLA_ROPE = 32
MLA_V = 64
ROPE_THETA_2 = 10000.0

MIX_WIDTH_2 = SSD_D_INNER + MLA_HEADS * MLA_V
IN_SSD = SSD_D_INNER + SSD_XBC + SSD_HEADS
IN_MLA = MLA_Q_RANK + MLA_KV_RANK + MLA_ROPE
IN_WIDTH_2 = IN_SSD + IN_MLA

MEM_HEADS = 4
MEM_HEAD_DIM = D_MODEL // MEM_HEADS

FFN_CONV = 3


def rmsnorm(x, w):
    xf = x.astype(jnp.float32)
    y = xf * lax.rsqrt(jnp.mean(xf * xf, axis=-1, keepdims=True) + EPS)
    return (y * w.astype(jnp.float32)).astype(x.dtype)

def causal_depthwise_conv(x, w, b):
    k = w.shape[0]
    y = lax.conv_general_dilated(
        x, w[:, None, :].astype(x.dtype), window_strides=(1,), padding=[(k - 1, 0)],
        dimension_numbers=("NWC", "WIO", "NWC"), feature_group_count=x.shape[-1])
    return y + b.astype(x.dtype)

def segsum_exp(a_cum):
    l = a_cum.shape[-1]
    diff = a_cum[..., :, None] - a_cum[..., None, :]
    mask = jnp.tril(jnp.ones((l, l), dtype=bool))
    return jnp.where(mask, jnp.exp(jnp.where(mask, diff, 0.0)), 0.0)

def rope_cos_sin(positions, dim):
    inv_freq = 1.0 / (ROPE_THETA_2 ** (jnp.arange(0, dim, 2, dtype=jnp.float32) / dim))
    ang = positions.astype(jnp.float32)[..., None] * inv_freq
    return jnp.cos(ang), jnp.sin(ang)

def apply_rope(t, cos, sin):
    t1, t2 = jnp.split(t.astype(jnp.float32), 2, axis=-1)
    return jnp.concatenate([t1 * cos - t2 * sin, t1 * sin + t2 * cos], axis=-1).astype(t.dtype)

def ssd_mixer(u, conv_w, conv_b, dt_bias, a_log, d_skip, norm_w):
    b, s, _ = u.shape
    nc = s // CHUNK
    e = SSD_HEADS // SSD_GROUPS
    z, xbc, dt = jnp.split(u, [SSD_D_INNER, SSD_D_INNER + SSD_XBC], axis=-1)
    xbc = jax.nn.silu(causal_depthwise_conv(xbc, conv_w, conv_b))
    xs, bm, cm = jnp.split(xbc, [SSD_D_INNER, SSD_D_INNER + SSD_GROUPS * SSD_STATE], axis=-1)
    xs = xs.reshape(b, nc, CHUNK, SSD_GROUPS, e, SSD_HEAD_DIM)
    bm = bm.reshape(b, nc, CHUNK, SSD_GROUPS, SSD_STATE)
    cm = cm.reshape(b, nc, CHUNK, SSD_GROUPS, SSD_STATE)
    dt = jax.nn.softplus(dt.astype(jnp.float32) + dt_bias.astype(jnp.float32))
    a = -jnp.exp(a_log.astype(jnp.float32))
    dt_c = dt.reshape(b, nc, CHUNK, SSD_GROUPS, e)
    a_dt = jnp.transpose(dt_c * a.reshape(SSD_GROUPS, e), (0, 3, 4, 1, 2))
    a_cum = jnp.cumsum(a_dt, axis=-1)
    x_dt = xs * dt_c[..., None]
    decay_in = segsum_exp(a_cum)
    cb = jnp.einsum("bclgn,bcsgn->bcgls", cm, bm)
    y_diag = jnp.einsum("bcgls,bgecls,bcsgep->bclgep", cb, decay_in, x_dt)
    decay_states = jnp.exp(a_cum[..., -1:] - a_cum)
    states = jnp.einsum("bclgn,bgecl,bclgep->bcgepn", bm, decay_states, x_dt)
    chunk_decay = jnp.exp(a_cum[..., -1])

    def step(h, inp):
        st, dec = inp
        return h * dec[..., None, None] + st, h

    h0 = jnp.zeros_like(states[:, 0])
    _, prev = lax.scan(step, h0, (jnp.moveaxis(states, 1, 0), jnp.moveaxis(chunk_decay, 3, 0)))
    prev = jnp.moveaxis(prev, 0, 1)
    y_off = jnp.einsum("bclgn,bcgepn,bgecl->bclgep", cm, prev, jnp.exp(a_cum))
    y = (y_diag + y_off).reshape(b, s, SSD_HEADS, SSD_HEAD_DIM)
    y = y + xs.reshape(b, s, SSD_HEADS, SSD_HEAD_DIM) * d_skip[:, None]
    y = y.reshape(b, s, SSD_D_INNER) * jax.nn.silu(z)
    y = rmsnorm(y.reshape(b, s, SSD_GROUPS, SSD_D_INNER // SSD_GROUPS),
                norm_w.reshape(SSD_GROUPS, SSD_D_INNER // SSD_GROUPS))
    return y.reshape(b, s, SSD_D_INNER).astype(u.dtype)

def mla_mixer(u, positions, q_norm_w, w_q_up, kv_norm_w, w_kv_up):
    b, s, _ = u.shape
    q_lat, kv_lat, k_rope = jnp.split(u, [MLA_Q_RANK, MLA_Q_RANK + MLA_KV_RANK], axis=-1)
    q = (rmsnorm(q_lat, q_norm_w) @ w_q_up).reshape(b, s, MLA_HEADS, MLA_NOPE + MLA_ROPE)
    q_nope, q_rope = jnp.split(q, [MLA_NOPE], axis=-1)
    kv = (rmsnorm(kv_lat, kv_norm_w) @ w_kv_up).reshape(b, s, MLA_HEADS, MLA_NOPE + MLA_V)
    k_nope, v = jnp.split(kv, [MLA_NOPE], axis=-1)
    cos, sin = rope_cos_sin(positions, MLA_ROPE)
    q_rope = apply_rope(q_rope, cos[:, :, None, :], sin[:, :, None, :])
    k_rope = apply_rope(k_rope, cos, sin)
    scale = (MLA_NOPE + MLA_ROPE) ** -0.5
    nb = s // Q_BLOCK
    k_chunk = jnp.arange(s) // CHUNK

    def blocks(t):
        return jnp.moveaxis(t.reshape(b, nb, Q_BLOCK, *t.shape[2:]), 1, 0)

    def attend(args):
        i, qn, qr = args
        sc = jnp.einsum("bqhd,bkhd->bhqk", qn, k_nope) + jnp.einsum("bqhr,bkr->bhqk", qr, k_rope)
        sc = sc.astype(jnp.float32) * scale
        q_chunk = (i * Q_BLOCK + jnp.arange(Q_BLOCK)) // CHUNK
        mask = k_chunk[None, :] <= q_chunk[:, None]
        sc = jnp.where(mask, sc, jnp.finfo(jnp.float32).min)
        p = jax.nn.softmax(sc, axis=-1).astype(v.dtype)
        return jnp.einsum("bhqk,bkhd->bqhd", p, v)

    o = lax.map(attend, (jnp.arange(nb), blocks(q_nope), blocks(q_rope)))
    return jnp.moveaxis(o, 0, 1).reshape(b, s, MLA_HEADS * MLA_V).astype(u.dtype)

def memory_attention(h, mem_h, wq, wk, wv, wo):
    b, s, _ = h.shape
    q = (h @ wq).reshape(b, s, MEM_HEADS, MEM_HEAD_DIM)
    k = (mem_h @ wk).reshape(b, -1, MEM_HEADS, MEM_HEAD_DIM)
    v = (mem_h @ wv).reshape(b, -1, MEM_HEADS, MEM_HEAD_DIM)
    sc = jnp.einsum("bqhd,bkhd->bhqk", q, k).astype(jnp.float32) * (MEM_HEAD_DIM ** -0.5)
    p = jax.nn.softmax(sc, axis=-1).astype(v.dtype)
    o = jnp.einsum("bhqk,bkhd->bqhd", p, v).reshape(b, s, D_MODEL)
    return o @ wo

def conv_ffn(h, w_up, conv_w, conv_b, w_down):
    u = causal_depthwise_conv(h @ w_up, conv_w, conv_b)
    g, val = jnp.split(u, 2, axis=-1)
    return (jax.nn.silu(g) * val) @ w_down

def second_inputs(seed: int = 0) -> dict:
    key = jax.random.key(seed)
    ks = iter(jax.random.split(key, 40))
    f32 = jnp.float32

    def dense(shape, fan_in):
        return jax.random.normal(next(ks), shape, f32) * (fan_in ** -0.5)

    def gain(shape):
        return 1.0 + 0.02 * jax.random.normal(next(ks), shape, f32)

    def small(shape):
        return 0.01 * jax.random.normal(next(ks), shape, f32)

    L = DEPTH
    x = jax.random.normal(next(ks), (BATCH, SEQ, D_MODEL), f32)
    mem = jax.random.normal(next(ks), (BATCH, N_MEM, D_MODEL), f32)
    offset = jax.random.randint(next(ks), (BATCH, 1), 0, 1024, dtype=jnp.int32)
    positions = offset + jnp.arange(SEQ, dtype=jnp.int32)[None, :]
    dt0 = jnp.exp(jax.random.uniform(next(ks), (L, SSD_HEADS), f32, np.log(1e-3), np.log(1e-1)))
    dt_bias = dt0 + jnp.log(-jnp.expm1(-dt0))
    a_log = jnp.log(jax.random.uniform(next(ks), (L, SSD_HEADS), f32, 1.0, 16.0))
    return {
        "x": x,
        "mem": mem,
        "positions": positions,
        "norm_mix_w": gain((L, D_MODEL)),
        "w_in": dense((L, D_MODEL, IN_WIDTH_2), D_MODEL),
        "ssd_conv_w": dense((L, SSD_CONV, SSD_XBC), SSD_CONV),
        "ssd_conv_b": small((L, SSD_XBC)),
        "ssd_dt_bias": dt_bias,
        "ssd_a_log": a_log,
        "ssd_d": 1.0 + 0.1 * jax.random.normal(next(ks), (L, SSD_HEADS), f32),
        "ssd_norm_w": gain((L, SSD_D_INNER)),
        "mla_q_norm_w": gain((L, MLA_Q_RANK)),
        "mla_w_q_up": dense((L, MLA_Q_RANK, MLA_HEADS * (MLA_NOPE + MLA_ROPE)), MLA_Q_RANK),
        "mla_kv_norm_w": gain((L, MLA_KV_RANK)),
        "mla_w_kv_up": dense((L, MLA_KV_RANK, MLA_HEADS * (MLA_NOPE + MLA_V)), MLA_KV_RANK),
        "w_out": dense((L, MIX_WIDTH_2, D_MODEL), MIX_WIDTH_2),
        "norm_memx_w": gain((L, D_MODEL)),
        "norm_mem_w": gain((L, D_MODEL)),
        "w_mem_q": dense((L, D_MODEL, D_MODEL), D_MODEL),
        "w_mem_k": dense((L, D_MODEL, D_MODEL), D_MODEL),
        "w_mem_v": dense((L, D_MODEL, D_MODEL), D_MODEL),
        "w_mem_o": dense((L, D_MODEL, D_MODEL), D_MODEL),
        "norm_ffn_w": gain((L, D_MODEL)),
        "w_ffn_up": dense((L, D_MODEL, 2 * D_FF), D_MODEL),
        "ffn_conv_w": dense((L, FFN_CONV, 2 * D_FF), FFN_CONV),
        "ffn_conv_b": small((L, 2 * D_FF)),
        "w_ffn_down": dense((L, D_FF, D_MODEL), D_FF),
        "norm_final_w": gain((D_MODEL,)),
    }

def second_block(x, mem, positions, norm_mix_w, w_in, ssd_conv_w, ssd_conv_b, ssd_dt_bias,
              ssd_a_log, ssd_d, ssd_norm_w, mla_q_norm_w, mla_w_q_up, mla_kv_norm_w,
              mla_w_kv_up, w_out, norm_memx_w, norm_mem_w, w_mem_q, w_mem_k, w_mem_v,
              w_mem_o, norm_ffn_w, w_ffn_up, ffn_conv_w, ffn_conv_b, w_ffn_down, norm_final_w):
    for l in range(DEPTH):
        h = rmsnorm(x, norm_mix_w[l])
        u = h @ w_in[l]
        u_ssd, u_mla = jnp.split(u, [IN_SSD], axis=-1)
        y_ssd = ssd_mixer(u_ssd, ssd_conv_w[l], ssd_conv_b[l], ssd_dt_bias[l], ssd_a_log[l],
                          ssd_d[l], ssd_norm_w[l])
        y_mla = mla_mixer(u_mla, positions, mla_q_norm_w[l], mla_w_q_up[l],
                          mla_kv_norm_w[l], mla_w_kv_up[l])
        x = x + jnp.concatenate([y_ssd, y_mla], axis=-1) @ w_out[l]
        x = x + memory_attention(rmsnorm(x, norm_memx_w[l]), rmsnorm(mem, norm_mem_w[l]),
                                 w_mem_q[l], w_mem_k[l], w_mem_v[l], w_mem_o[l])
        x = x + conv_ffn(rmsnorm(x, norm_ffn_w[l]), w_ffn_up[l], ffn_conv_w[l], ffn_conv_b[l],
                         w_ffn_down[l])
    return rmsnorm(x, norm_final_w)


def setup_inputs(seed=0):
    out = dict(first_inputs(seed))
    for name, value in second_inputs(seed + 1).items():
        if name != "x":
            out[name + "_2"] = value
    return out


def reference(
    x, positions, ffn1_pre, ffn1_w_gu, ffn1_w_down, ffn1_post, mix_pre, w_in, w_pool,
    pool_scale, sinks, g_pool, g_attn, w_out, mix_post, ffn2_pre, ffn2_w_gu, ffn2_w_down,
    ffn2_post, mem_2, positions_2, norm_mix_w_2, w_in_2, ssd_conv_w_2, ssd_conv_b_2,
    ssd_dt_bias_2, ssd_a_log_2, ssd_d_2, ssd_norm_w_2, mla_q_norm_w_2, mla_w_q_up_2,
    mla_kv_norm_w_2, mla_w_kv_up_2, w_out_2, norm_memx_w_2, norm_mem_w_2, w_mem_q_2, w_mem_k_2,
    w_mem_v_2, w_mem_o_2, norm_ffn_w_2, w_ffn_up_2, ffn_conv_w_2, ffn_conv_b_2, w_ffn_down_2,
    norm_final_w_2,
):
    x = first_block(
        x, positions, ffn1_pre, ffn1_w_gu, ffn1_w_down, ffn1_post, mix_pre, w_in, w_pool,
        pool_scale, sinks, g_pool, g_attn, w_out, mix_post, ffn2_pre, ffn2_w_gu, ffn2_w_down,
        ffn2_post,
    )
    return second_block(
        x, mem_2, positions_2, norm_mix_w_2, w_in_2, ssd_conv_w_2, ssd_conv_b_2, ssd_dt_bias_2,
        ssd_a_log_2, ssd_d_2, ssd_norm_w_2, mla_q_norm_w_2, mla_w_q_up_2, mla_kv_norm_w_2,
        mla_w_kv_up_2, w_out_2, norm_memx_w_2, norm_mem_w_2, w_mem_q_2, w_mem_k_2, w_mem_v_2,
        w_mem_o_2, norm_ffn_w_2, w_ffn_up_2, ffn_conv_w_2, ffn_conv_b_2, w_ffn_down_2,
        norm_final_w_2,
    )


_drawn_inputs = setup_inputs


def setup_inputs(seed=0):
    import zlib

    import numpy as np

    out = dict(_drawn_inputs(seed))
    spreads = {}
    factors = {'sinks': 5.391,
     'ffn2_post': 3.181,
     'norm_mix_w_2': 4.384,
     'ssd_conv_b_2': 8.0,
     'ssd_norm_w_2': 6.729,
     'mla_q_norm_w_2': 8.0,
     'mla_kv_norm_w_2': 8.0,
     'norm_memx_w_2': 8.0,
     'norm_mem_w_2': 8.0,
     'norm_ffn_w_2': 6.183,
     'ffn_conv_b_2': 26.319,
     'norm_final_w_2': 22.069,
     'ssd_d_2': 24.293}
    for name, (base, spread) in spreads.items():
        noise = np.random.default_rng([zlib.crc32(name.encode()), seed]).standard_normal(out[name].shape)
        drawn = base * np.exp(spread * noise) if base else spread * noise
        out[name] = __import__('jax').numpy.asarray(drawn.astype(out[name].dtype))
    for name, factor in factors.items():
        out[name] = (out[name] * factor).astype(out[name].dtype)
    return out
```

```python
from contextlib import ExitStack

import numpy as np

import concourse.bass as bass
from concourse import mybir

F32 = mybir.dt.float32
F32R = mybir.dt.float32r
BF16 = mybir.dt.bfloat16
I32 = mybir.dt.int32
ACT = mybir.ActivationFunctionType
ALU = mybir.AluOpType
AX = mybir.AxisListType

P = 128
TT = 2
S = TT * P
D = 1024
KT = D // P
DFF = 2816
EPS = 1e-6
NEG = -1e30

POOL_WINDOWS = (2, 4, 8, 16)
PW = 512
HEADS, HD = 8, 64
THETA1, ROT1 = 500000.0, 16
SH, SP_, SG, SN = 16, 64, 4, 128
THETA2, ROT2 = 10000.0, 32
MH, NOPE, ROPE, MV = 16, 64, 32, 64
QK = NOPE + ROPE
QR, KVR = 384, 256
IN2 = 3760
XBC0, TAIL0 = 1024, 3072
TAILW = IN2 - TAIL0
T_DT, T_Q, T_KV, T_KR = 0, 16, 16 + QR, 16 + QR + KVR
MEMH, MEMD = 4, 256

FC = 256
NCH = DFF // FC

RING = 3
UW = 2048
LAYERS = [("f0", 3 * NCH), ("win", 5), ("wout", 4), ("f1", 3 * NCH), ("in2", 15), ("out_ssd", 4),
          ("qup", 3), ("kvup", 2), ("out_mla", 4), ("mk", 4), ("mv", 4), ("mq", 4), ("mo", 4),
          ("f2", 3 * NCH)]
U0, _n = {}, 0
for _name, _k in LAYERS:
    U0[_name] = _n
    _n += _k
UNITS = _n

NORMS = [("f0", (1024,)), ("win", (1024,)), ("wout", (512, 512)), ("f1", (1024,)), ("in2", (1024,)),
         ("out_ssd", (256,) * 4), ("mla", (QR, KVR)), ("out_mla", None), ("mk", (1024,)),
         ("mq", (1024,)), ("mo", None), ("f2", (1024,))]
NIDX = {n: i for i, (n, _) in enumerate(NORMS)}

GROUPS = [("swa", g, (1, 2), 4, HD) for g in range(2)] + [("mla", g, (1, 2), 4, MV) for g in range(4)] \
    + [("mem", g, (2, 2), 2, MEMD) for g in range(2)]

ROWS, _at = {}, {0: 0, 1: 0, 2: 0, 3: 0}
for _name, _tile, _k in [("ffn1_pre", 0, 8), ("mix_pre", 0, 8), ("ffn2_pre", 0, 8), ("norm_mix_w_2", 0, 8),
                         ("norm_memx_w_2", 0, 8), ("norm_mem_w_2", 0, 8), ("norm_ffn_w_2", 0, 8),
                         ("mla_q_norm_w_2", 0, 3), ("mla_kv_norm_w_2", 0, 2), ("g_pool", 0, 4),
                         ("g_attn", 0, 4), ("ssd_norm_w_2", 0, 8),
                         ("ssd_conv_w_2", 1, 64), ("ssd_conv_b_2", 1, 16)]:
    ROWS[_name] = (_tile, _at[_tile], _k)
    _at[_tile] += _k
ROW_TILES = [_at[0], _at[1], 128, 48]
COL_AT = [0, ROW_TILES[0], ROW_TILES[0] + ROW_TILES[1], ROW_TILES[0] + ROW_TILES[1] + 128]
NCOLS = COL_AT[3] + 48
FCONV = COL_AT[2]
GAIN = {"f0": "ffn1_pre", "win": "mix_pre", "wout": "g_pool", "f1": "ffn2_pre", "in2": "norm_mix_w_2",
        "out_ssd": "ssd_norm_w_2", "mla": "mla_q_norm_w_2", "mk": "norm_mem_w_2", "mq": "norm_memx_w_2",
        "f2": "norm_ffn_w_2"}


def col(name):
    t, r, _ = ROWS[name]
    return COL_AT[t] + r


C_ID, C_TRI, C_GT, C_BAND, C_MASK, C_FREQ = 0, 128, 256, 384, 384 + 4 * 384, 384 + 4 * 384 + 256
NFREQ = ROT1 // 2 + ROT2 // 2
C_N = C_FREQ + NFREQ


def constants():
    c = np.zeros((P, C_N), np.float32)
    i = np.arange(P)
    c[:, C_ID:C_ID + P] = np.eye(P)
    c[:, C_TRI:C_TRI + P] = i[:, None] <= i[None, :]
    c[:, C_GT:C_GT + P] = i[:, None] > i[None, :]
    t = np.arange(S)
    for g, w in enumerate(POOL_WINDOWS):
        m = ((t[:, None] <= t[None, :]) & (t[:, None] > t[None, :] - w)) / np.minimum(t + 1, w)[None, :]
        m = m - np.eye(S)
        at = C_BAND + g * 384
        c[:, at:at + S] = m[:P]
        c[:, at + S:at + 384] = m[P:, P:]
    c[:, C_MASK:C_MASK + P] = np.where(i[None, :] > i[:, None], 0.0, NEG)
    c[:, C_MASK + P:C_MASK + 2 * P] = np.where(i[None, :] <= i[:, None], 0.0, NEG)
    f1 = THETA1 ** (-np.arange(0, ROT1, 2) / ROT1)
    f2 = 1.0 / (THETA2 ** (np.arange(0, ROT2, 2) / ROT2))
    c[:, C_FREQ:C_FREQ + NFREQ] = np.concatenate([f1, f2])[None, :]
    q = np.zeros((2, MH, S), np.float32)
    k = np.zeros((2, MH, S), np.float32)
    for t in range(TT):
        q[t, :, t * P:t * P + 64] = 1.0
        k[t, :, t * P + 64:(t + 1) * P] = NEG
    return c, np.stack([q, k]).reshape(2, 2, MH * S)


def two_blocks(nc, a, consts, mla_rows, out):
    with ExitStack() as ctx:
        def sb(name, shape, dt=F32):
            return ctx.enter_context(nc.sbuf_tensor(name, shape, dt))

        def sem(name):
            return ctx.enter_context(nc.semaphore(name))

        raw = [sb(f"raw{i}", [P, UW]) for i in range(RING)]
        w_hi = [sb(f"w_hi{i}", [P, UW], F32R) for i in range(RING)]
        w_lo = [sb(f"w_lo{i}", [P, UW], F32R) for i in range(RING)]
        X = sb("X", [P, TT, D])
        xs = sb("xs", [P, TT, D])
        xT_hi = sb("xT_hi", [P, KT, S], F32R)
        xT_lo = sb("xT_lo", [P, KT, S], F32R)
        hT_hi = sb("hT_hi", [P, 2, S], F32R)
        hT_lo = sb("hT_lo", [P, 2, S], F32R)
        xd_end = sb("xd_end", [P, D])
        gain_row = sb("gain_row", [P, D])
        cst = sb("cst", [P, C_N])
        cols = sb("cols", [P, NCOLS])
        ident_bf = sb("ident_bf", [P, P], BF16)
        mask_bf = sb("mask_bf", [P, 2 * P], BF16)
        ssq = sb("ssq", [P, TT, 4])
        rstd = sb("rstd", [P, TT, 4])
        post_ssq = sb("post_ssq", [P, TT])
        post_rstd = sb("post_rstd", [P, TT])
        neg_half = sb("neg_half", [P, TT * 4])
        pos_i = sb("pos_i", [P, 2, TT], I32)
        pos_f = sb("pos_f", [P, 2, TT])
        NA = TT * NFREQ
        ang = sb("ang", [P, 2, TT, NFREQ])
        turns = sb("turns", [P, 2, TT, NFREQ])
        trig = sb("trig", [P, 2, TT, NFREQ])
        sink_row = sb("sink_row", [P, HEADS])
        head_rows = sb("head_rows", [P, 3, SH])
        mx = sb("mx", [P, TT, 4])
        neg_max = sb("neg_max", [P, 2, TT, 4])
        sink_arg = sb("sink_arg", [P, 2, TT, 4])
        sink_exp = sb("sink_exp", [P, 2, TT, 4])
        p_sum = sb("p_sum", [P, 2, TT, 4])
        den = sb("den", [P, 2, TT, 4])
        rec = sb("rec", [P, 2, TT, 4])
        conv_now = sb("conv_now", [P, 8, 2])
        k_rope = sb("k_rope", [P, TT, ROPE])
        sm = sb("sm", [P, 12, TT * SH])
        arena = sb("arena", [P, 18464])

        def view(at, *dims):
            v = arena[:, at:at + int(np.prod(dims))]
            if len(dims) == 2:
                return v.rearrange("p (a b) -> p a b", a=dims[0])
            if len(dims) == 3:
                return v.rearrange("p (a b c) -> p a b c", a=dims[0], b=dims[1])
            return v

        rows = view(0, 4, P)
        act_in = view(0, TT, 512)
        conv_y = view(1024, 4, S)
        silu_g = view(2048, 2, 256)
        act_s = view(2560, 2, 256)
        z1 = view(0, TT, 1280)
        k_pad = view(2560, TT, 4, P)
        qT1 = view(3584, 4, S)
        kT1 = view(4608, 4, S)
        dT = view(5632, 4, S)
        pool_y = view(6656, TT, PW)
        o1 = view(7680, TT, PW)
        w_pool_sb = view(8704, 4, P)
        pool_scale = view(9216, 512)
        zg = view(0, TT, D)
        tail = view(2048, TT, TAILW)
        xbcT = view(3424, 16, S)
        xbc_in = [view(7520 + i * 1024, TT, 512) for i in range(2)]
        xs_tok = view(7520, TT, D)
        conv_x = view(9568, 4, S)
        xdt = view(9568, TT, D)
        steps = view(11616, SH, P)
        decay = [view(13664 + i * 512, 4, P) for i in range(2)]
        cbm = view(14688, SG, 3 * P)
        y_ssd = view(16224, TT, D)
        q_tok = view(0, TT, MH, QK)
        k_tok = view(3072, TT, MH, QK)
        v_tok = view(6144, TT, MH * MV)
        qT2 = view(8192, MH, S)
        kT2 = view(12288, MH, S)
        o2 = view(16384, TT, D)
        mem_x = view(0, TT, D)
        m_tok = view(2048, TT, D)
        kT3 = view(4096, KT, S)
        v3 = view(6144, TT, D)
        qT3 = view(8192, KT, S)
        o3 = view(10240, TT, D)
        PROB = {"swa": (9728, 12800, 1536), "mla": (0, 3072, 1536), "mem": (12288, 14336, 1024)}

        def prob(gi):
            at, _, n = PROB[GROUPS[gi][0]]
            return view(at + gi % 2 * n, n)

        def prob_T(gi):
            _, at, n = PROB[GROUPS[gi][0]]
            return view(at + gi % 2 * n, n)

        ps = ctx.enter_context(nc.psum_tensor("ps", [P, 8, 512], F32))
        dn = ps[:, 4:8, :].rearrange("p (t h) n -> p t (h n)", t=TT)

        def banks(b, n):
            return ps[:, b:b + n, :].rearrange("p b n -> p (b n)")

        ident = cst[:, C_ID:C_ID + P]
        tri = cst[:, C_TRI:C_TRI + P]
        later = cst[:, C_GT:C_GT + P]
        ident_n = lambda n: cst[0:n, C_ID:C_ID + n]
        def bc(ap, n):
            return ap.unsqueeze(ap.ndim).broadcast_to(list(ap.shape) + [n])

        def bh(ap, n):
            return ap.unsqueeze(1).broadcast_to([ap.shape[0], n] + list(ap.shape[1:]))

        weights_in = [sem(f"weights_in{i}") for i in range(RING)]
        (rounded, resid, unit_used) = map(sem, ("rounded", "resid", "unit_used"))
        (x_in, small_in, pos_in, rows_in, gain_in, mem_in, mask_rows_in, out_written) = map(sem, (
            "x_in", "small_in", "pos_in", "rows_in", "gain_in", "mem_in", "mask_rows_in", "out_written"))
        (cols_ps, cols_ready, consts_bf, half_ready) = map(sem, ("cols_ps", "cols_ready", "consts_bf", "half_ready"))
        (ang_ready, trig_ready) = map(sem, ("ang_ready", "trig_ready"))
        (ssq_done, rstd_done, scaled, xt_ps, xt_hi, xt_lo) = map(sem, (
            "ssq_done", "rstd_done", "scaled", "xt_ps", "xt_hi", "xt_lo"))
        (gu_ps, silu_done, s_ready, hT_ps, hT_hi_done, hT_lo_done) = map(sem, (
            "gu_ps", "silu_done", "s_ready", "hT_ps", "hT_hi_done", "hT_lo_done"))
        (u_ready, uT_ps, taps_ready, tap2, tap1, tap0, conv_silu, conv_s) = map(sem, (
            "u_ready", "uT_ps", "taps_ready", "tap2", "tap1", "tap0", "conv_silu", "conv_s"))
        (post_ssq_done, post_rstd_done, post_t, x_ready) = map(sem, (
            "post_ssq_done", "post_rstd_done", "post_t", "x_ready"))
        (z1_act, z1_dve, dT_ps, dT_ready, pool_ps, pool_ready) = map(sem, (
            "z1_act", "z1_dve", "dT_ps", "dT_ready", "pool_ps", "pool_ready"))
        (rope1_done, k_pad_done, qT1_ps, kT1_ps, qT1_ready, kT1_ready) = map(sem, (
            "rope1_done", "k_pad_done", "qT1_ps", "kT1_ps", "qT1_ready", "kT1_ready"))
        (sc_ps, negm_ready, p_ready, pT_ps, pT_ready, o_ps, o_ready) = map(sem, (
            "sc_ps", "negm_ready", "p_ready", "pT_ps", "pT_ready", "o_ps", "o_ready"))
        (in2_act, in2_dve, xbT_ps, conv_first, conv_tap, xbc_ready) = map(sem, (
            "in2_act", "in2_dve", "xbT_ps", "conv_first", "conv_tap", "xbc_ready"))
        (dt_arg, dt_exp, adt_ready, dt_ready, cum_ps, cum_exp, cb_ps, cbm_ready) = map(sem, (
            "dt_arg", "dt_exp", "adt_ready", "dt_ready", "cum_ps", "cum_exp", "cb_ps", "cbm_ready"))
        (xs_ps, xs_tok_ready, xdt_ready, skip_ready, xd_end_ready, steps_ready, dm_ps, dm_exp, dm_masked, y_ps,
         off_ps, y_ready) = map(sem, ("xs_ps", "xs_tok_ready", "xdt_ready", "skip_ready", "xd_end_ready",
                                      "steps_ready", "dm_ps", "dm_exp", "dm_masked", "y_ps", "off_ps", "y_ready"))
        (q2_act, q2_dve, kv_ps, kv_act, kv_dve, k_rope_done, k_rope_spread, rope2_done, mT_ps, mT_act,
         mT_dve) = map(sem, ("q2_act", "q2_dve", "kv_ps", "kv_act", "kv_dve", "k_rope_done",
                             "k_rope_spread", "rope2_done", "mT_ps", "mT_act", "mT_dve"))
        (m_act, m_dve, m3_ps, m3_act, m3_dve) = map(sem, ("m_act", "m_dve", "m3_ps", "m3_act", "m3_dve"))
        (act_step, dve_step, pool_step) = map(sem, ("act_step", "dve_step", "pool_step"))

        def kt_of(name):
            parts = dict(NORMS)[name]
            return -(-sum(parts) // P) if parts else KT

        def kts(name, k=0):
            i = NIDX[name]
            return sum(kt_of(n) for n, _ in NORMS[:i]) + k

        REAL = [n for n, p in NORMS if p]

        def parts_done(name):
            return sum(TT * len(dict(NORMS)[n]) for n in REAL[:REAL.index(name) + 1])

        END = {name: U0[name] + n for name, n in LAYERS}
        XU = ["f0", "wout", "f1", "out_ssd", "out_mla", "mo", "f2"]
        POST = ["f0", "wout", "f1", "final"]
        XS_OF = {"f0": 0, "win": 1, "f1": 2, "in2": 3, "mq": 5, "f2": 6}

        def width(u):
            if u == U0["in2"] + 10:
                return 8 * (IN2 - 3584)
            if U0["qup"] <= u < U0["kvup"]:
                return 3 * 512
            return UW

        mem_parts = {"f0": [X], "win": [X], "f1": [X], "in2": [X], "mq": [X], "f2": [X], "mk": [mem_x],
                     "wout": [pool_y, o1], "out_ssd": [y_ssd[:, :, g * 256:(g + 1) * 256] for g in range(4)],
                     "mla": [tail[:, :, T_Q:T_Q + QR], tail[:, :, T_KV:T_KV + KVR]]}

        IN2_CHUNKS = [2, 3, 4, 5, 6, 7, 0, 1]

        def in2_unit0(n):
            return U0["in2"] + (2 * n if n <= 5 else 2 * n - 1)

        block = ctx.enter_context(nc.Block())

        @block.sync
        def _(sp):
            def load(k, dst_src, c=0):
                if not isinstance(c, int) or k + 3 * c >= RING:
                    sp.wait_ge(resid, 3 * c + (k - RING + 1))
                for dst, src in dst_src:
                    sp.dma_start(dst, src).then_inc(weights_in[k % RING], 16)

            def rows_by_cols(k, w, row_tile, nk, c0, n):
                src = w.rearrange("(k p) n -> p k n", p=P)
                dst = raw[k % RING][:, 0:nk * n].rearrange("p (k n) -> p k n", k=nk)
                h = (nk + 1) // 2
                return [(dst[:, 0:h], src[:, row_tile:row_tile + h, c0:c0 + n]),
                        (dst[:, h:nk], src[:, row_tile + h:row_tile + nk, c0:c0 + n])]

            def gate_up(k, w, half, c):
                src = w.rearrange("(k p) (g n) -> p k g n", p=P, g=2)
                dst = raw[k % RING][:, :].rearrange("p (k g n) -> p k g n", k=4, g=2)
                return [(dst[:, :, g], src[:, 4 * half:4 * half + 4, g, bass.ds(c * FC, FC)]) for g in range(2)]

            def down(k, w, c):
                src = w.rearrange("(c k p) n -> c k p n", k=2, p=P)
                dst = raw[k % RING][:, :].rearrange("p (k n) -> p k n", k=2)
                rows_ = w.rearrange("(c p) n -> p c n", p=P)
                return [(dst[:, j], rows_[:, bass.ds(2 * c + j, 1), :].rearrange("p c n -> p (c n)")) for j in range(2)]

            def feed_forward(name, gu, dw):
                u = U0[name]
                load(u, gate_up(u, gu, 0, 0))
                load(u + 1, gate_up(u + 1, gu, 1, 0))
                load(u + 2, gate_up(u + 2, gu, 0, 1))
                load(u + 3, gate_up(u + 3, gu, 1, 1))
                load(u + 4, down(u + 4, dw, 0))
                with sp.Fori(0, NCH - 2) as j:
                    load(u + 5, gate_up(u + 5, gu, 0, j + 2), j)
                    load(u + 6, gate_up(u + 6, gu, 1, j + 2), j)
                    load(u + 7, down(u + 7, dw, j + 1), j)
                k = u + 3 * NCH - 1
                load(k, down(k, dw, NCH - 1))

            def two_row_tiles(name, w, first=0):
                for i in range(4):
                    k = U0[name] + i
                    load(k, rows_by_cols(k, w, first + 2 * i, 2, 0, D))

            feed_forward("f0", a["ffn1_w_gu"][0], a["ffn1_w_down"][0])
            for i in range(4):
                k = U0["win"] + i
                load(k, rows_by_cols(k, a["w_in"][0], 4 * (i % 2), 4, 512 * (i // 2), 512))
            k = U0["win"] + 4
            load(k, rows_by_cols(k, a["w_in"][0], 0, 8, 1024, 256))
            two_row_tiles("wout", a["w_out"][0])
            feed_forward("f1", a["ffn2_w_gu"][0], a["ffn2_w_down"][0])
            for n, c in enumerate(IN2_CHUNKS):
                k = in2_unit0(n)
                if c == 7:
                    load(k, rows_by_cols(k, a["w_in_2"][0], 0, 8, 3584, IN2 - 3584))
                else:
                    for half in range(2):
                        load(k + half, rows_by_cols(k + half, a["w_in_2"][0], 4 * half, 4, 512 * c, 512))
            two_row_tiles("out_ssd", a["w_out_2"][0])
            for i in range(3):
                k = U0["qup"] + i
                load(k, rows_by_cols(k, a["mla_w_q_up_2"][0], 0, 3, 512 * i, 512))
            for i in range(2):
                k = U0["kvup"] + i
                load(k, rows_by_cols(k, a["mla_w_kv_up_2"][0], 0, 2, 1024 * i, 1024))
            two_row_tiles("out_mla", a["w_out_2"][0], 8)
            two_row_tiles("mk", a["w_mem_k_2"][0])
            two_row_tiles("mv", a["w_mem_v_2"][0])
            two_row_tiles("mq", a["w_mem_q_2"][0])
            two_row_tiles("mo", a["w_mem_o_2"][0])
            feed_forward("f2", a["w_ffn_up_2"][0], a["w_ffn_down_2"][0])
            for t in range(TT):
                sp.wait_ge(x_ready, 2 * len(XU) + t + 1)
                sp.dma_start(out[0].rearrange("(t p) n -> p t n", p=P)[:, t, :], xs[:, t, :]).then_inc(out_written, 16)
            sp.wait_ge(out_written, 16 * TT)

        @block.scalar
        def _(act):
            steps_n = [0]

            def link(ins):
                steps_n[0] += 1
                ins.then_inc(act_step, 1)
                act.wait_ge(act_step, steps_n[0])

            xv = a["x"][0].rearrange("(t p) n -> p t n", p=P)
            for t in range(TT):
                act.dma_start(X[:, t, :], xv[:, t, :]).then_inc(x_in, 16)
            act.dma_start(cst[:, :], consts).then_inc(small_in, 16)
            for name, (t, r, n) in ROWS.items():
                src = a[name]
                if len(src.shape) == 3:
                    src = src.rearrange("l a n -> l (a n)")
                act.dma_start(rows[r:r + n, t, :], src[0].rearrange("(r n) -> r n", n=P)).then_inc(rows_in, 16)
            cw = a["ffn_conv_w_2"].rearrange("l a n -> l (a n)")[0].rearrange("(r n) -> r n", n=P)
            act.dma_start(rows[:, 2, :], cw[0:P, :]).then_inc(rows_in, 16)
            act.dma_start(rows[0:4, 3, :], cw[P:132, :]).then_inc(rows_in, 16)
            act.dma_start(rows[4:48, 3, :], a["ffn_conv_b_2"][0].rearrange("(r n) -> r n", n=P)).then_inc(rows_in, 16)
            for i, name in enumerate(["positions", "positions_2"]):
                act.dma_start(pos_i[:, i, :], a[name][0].rearrange("(t p) -> p t", p=P),
                              allow_slow_non_contiguous=True).then_inc(pos_in, 16)
            act.dma_start(sink_row[:, :], a["sinks"][0].partition_broadcast(P)).then_inc(small_in, 16)
            for i, name in enumerate(["ssd_dt_bias_2", "ssd_a_log_2", "ssd_d_2"]):
                act.dma_start(head_rows[:, i, :], a[name][0].partition_broadcast(P)).then_inc(small_in, 16)
            act.dma_start(w_pool_sb[:, :, :], a["w_pool"][0].rearrange("g c d -> c g d")).then_inc(small_in, 16)
            act.dma_start(pool_scale[:, :], a["pool_scale"][0].partition_broadcast(P)).then_inc(small_in, 16)

            def split(k, c=0):
                if isinstance(c, int) and k + 3 * c >= UNITS:
                    return
                n = width(k) if isinstance(c, int) else UW
                act.wait_ge(weights_in[k % RING], 32 * c + 32 * (k // RING + 1))
                if not isinstance(c, int) or k + 3 * c >= RING:
                    act.wait_ge(unit_used, 3 * c + (k - RING + 1))
                act.activation(w_hi[k % RING][:, 0:n], raw[k % RING][:, 0:n], ACT.Copy).then_inc(rounded, 1)

            def norm(name):
                parts = dict(NORMS)[name]
                if parts:
                    if name in XS_OF and XS_OF[name]:
                        act.wait_ge(x_ready, 2 * XS_OF[name])
                    for i, src in enumerate(mem_parts[name]):
                        n, at = parts[i], sum(parts[:i])
                        for t in range(TT):
                            act.activation(xs[:, t, at:at + n], src[:, t, :], ACT.Square, scale=float(n) ** -0.5,
                                           accum_out=ssq[:, t, i:i + 1]).then_inc(ssq_done, 1)
                for k in range(kt_of(name)):
                    act.wait_ge(xt_ps, kts(name, min(k // 2 * 2 + 2, kt_of(name))))
                    src = ps[:, k // 2, k % 2 * S:k % 2 * S + S]
                    if parts:
                        g = col(GAIN[name]) + k
                        act.activation(xT_hi[:, k, :], src, ACT.Copy, scale=cols[:, g:g + 1]).then_inc(xt_hi, 1)
                    else:
                        act.activation(xT_hi[:, k, :], src, ACT.Copy).then_inc(xt_hi, 1)

            def post(name):
                i = POST.index(name)
                if name == "final":
                    act.wait_ge(x_ready, 2 * len(XU))
                else:
                    act.wait_ge(unit_used, END[name])
                src = X if name == "final" else dn
                for t in range(TT):
                    act.activation(xs[:, t, :], src[:, t, :], ACT.Square, scale=float(D) ** -0.5,
                                   accum_out=post_ssq[:, t:t + 1]).then_inc(post_ssq_done, 1)

            def chunk(f, conv, k, c, peeled):
                j = c if peeled is None else 0
                fc = f * NCH + (peeled if peeled is not None else 2)
                split(k + 2, j)
                split(k + 3, j)
                for t in range(TT):
                    if t == 0:
                        act.wait_ge(gu_ps, j + (fc + 1))
                    else:
                        act.wait_ge(unit_used, 3 * j + (k + 2))
                    if conv:
                        act.activation(act_in[:, t, :], ps[:, t, :], ACT.Copy).then_inc(u_ready, 1)
                    else:
                        act.activation(silu_g[:, t, :], ps[:, t, 0:FC], ACT.Silu).then_inc(silu_done, 1)
                if peeled != 0:
                    split(k + 4, j)
                if conv:
                    n = fc - 2 * NCH
                    act.wait_ge(uT_ps, j + (n + 1))
                    act.wait_ge(taps_ready, j + (n + 1))
                    for q in range(4):
                        act.activation(conv_y[:, q, :], ps[:, 2 + q // 2, q % 2 * S:q % 2 * S + S], ACT.Identity,
                                       bias=conv_now[:, 6 + q // 2, q % 2:q % 2 + 1],
                                       scale=conv_now[:, 4 + q // 2, q % 2:q % 2 + 1]).then_inc(tap2, 1)
                    act.wait_ge(tap0, 4 * j + (4 * n + 4))
                    act.activation(silu_g[:, :, :], conv_y[:, 0:2, :], ACT.Silu).then_inc(conv_silu, 1)
                    act.wait_ge(conv_s, j + (n + 1))
                    act.activation(hT_hi[:, :, :], act_s[:, :, :], ACT.Copy).then_inc(hT_hi_done, 1)
                else:
                    act.wait_ge(hT_ps, j + (fc + 1))
                    act.activation(hT_hi[:, :, :].rearrange("p a b -> p (a b)"), ps[:, 2, :],
                                   ACT.Copy).then_inc(hT_hi_done, 1)

            def feed_forward(f, conv):
                name = f"f{f}"
                u = U0[name]
                norm(name)
                chunk(f, conv, u, 0, 0)
                chunk(f, conv, u + 2, 0, 1)
                with act.Fori(0, NCH - 3) as j:
                    chunk(f, conv, u + 5, j, None)
                chunk(f, conv, u + 3 * NCH - 4, 0, NCH - 1)
                split(u + 3 * NCH + 1)

            def dense(name, units):
                for i in range(units):
                    split(U0[name] + i + 2)

            def exps(gi):
                kind, g, nk, hg, dv = GROUPS[gi]
                scale = {"swa": HD ** -0.5, "mla": QK ** -0.5, "mem": MEMD ** -0.5}[kind]
                at = 0
                b = gi % 2
                if gi >= 2:
                    act.wait_ge(pT_ps, gi - 1)
                for t in range(TT):
                    act.wait_ge(negm_ready, 2 * gi + t + 1)
                    n = nk[t] * P
                    for h in range(hg):
                        last = act.activation(prob(gi)[:, at:at + n], banks(0, 3)[:, at:at + n], ACT.Exp,
                                              bias=neg_max[:, b, t, h:h + 1], scale=scale,
                                              accum_out=p_sum[:, b, t, h:h + 1])
                        if h < hg - 1 or kind == "swa":
                            pass
                        at += n
                    if kind == "swa":
                        act.activation(sink_exp[:, b, t, :], sink_arg[:, b, t, :], ACT.Exp).then_inc(p_ready, 1)
                    else:
                        last.then_inc(p_ready, 1)

            def attention(first, n):
                exps(first)
                for gi in range(first + 1, first + n):
                    exps(gi)

            act.wait_ge(cols_ps, 1)
            act.activation(cols[:, :], ps[:, 7, 0:NCOLS], ACT.Copy).then_inc(cols_ready, 1)
            act.wait_ge(ang_ready, 1)
            act.activation(trig[:, :, :, :], ang[:, :, :, :], ACT.Sin).then_inc(trig_ready, 1)
            split(0)
            split(1)
            act.wait_ge(x_in, 32)
            feed_forward(0, False)
            post("f0")

            norm("win")
            for n in range(3):
                for i in range(2 if n < 2 else 1):
                    split(U0["win"] + 2 * n + i + 2)
                act.wait_ge(unit_used, min(U0["win"] + 2 * n + 2, END["win"]))
                w = 512 if n < 2 else 256
                act.activation(z1[:, 0, 512 * n:512 * n + w], ps[:, 2 * n, 0:w], ACT.Copy).then_inc(z1_act, 1)
            act.wait_ge(dT_ps, 1)
            act.activation(dT[:, :, :].rearrange("p a b -> p (a b)"), banks(6, 2), ACT.Copy).then_inc(dT_ready, 1)
            act.wait_ge(qT1_ps, 1)
            act.activation(qT1[:, :, :].rearrange("p a b -> p (a b)"), banks(2, 2), ACT.Copy).then_inc(qT1_ready, 1)
            attention(0, 2)
            act.wait_ge(o_ready, 2)
            act.wait_ge(pool_ready, 2)
            norm("wout")
            dense("wout", 4)
            post("wout")
            feed_forward(1, False)
            post("f1")

            norm("in2")
            for n, c in enumerate(IN2_CHUNKS):
                for i in range(1 if c == 7 else 2):
                    split(in2_unit0(n) + i + 2)
                act.wait_ge(unit_used, in2_unit0(n) + (1 if c == 7 else 2))
                b = n % 2 * 2
                if n < 4:
                    if n >= 2:
                        act.wait_ge(xbT_ps, n - 1)
                    act.activation(xbc_in[n % 2][:, 0, :], ps[:, b, :], ACT.Copy).then_inc(in2_act, 1)
                elif c == 6:
                    act.activation(tail[:, 0, 0:512], ps[:, b, :], ACT.Copy).then_inc(in2_act, 1)
                elif c == 7:
                    act.activation(tail[:, 0, 512:TAILW], ps[:, b, 0:TAILW - 512], ACT.Copy).then_inc(in2_act, 1)
                else:
                    act.activation(zg[:, 0, 512 * c:512 * c + 512], ps[:, b, :], ACT.Silu)
                    act.activation(zg[:, 1, 512 * c:512 * c + 512], ps[:, b + 1, :], ACT.Silu).then_inc(in2_act, 1)
                if 1 <= n <= 4:
                    m = n - 1
                    act.wait_ge(xbT_ps, m + 1)
                    if m:
                        act.wait_ge(xbc_ready, m)
                    for q in range(4):
                        ft = 4 * m + q
                        act.activation(conv_x[:, q, :], ps[:, 4 + m % 2 * 2 + q // 2, q % 2 * S:q % 2 * S + S],
                                       ACT.Identity, bias=cols[:, col("ssd_conv_b_2") + ft:col("ssd_conv_b_2") + ft + 1],
                                       scale=cols[:, col("ssd_conv_w_2") + 48 + ft:col("ssd_conv_w_2") + 49 + ft])\
                           .then_inc(conv_first, 1)
                    act.wait_ge(conv_tap, 12 * (m + 1))
                    act.activation(xbcT[:, 4 * m:4 * m + 4, :], conv_x[:, :, :], ACT.Silu).then_inc(xbc_ready, 1)
            act.wait_ge(dt_arg, 1)
            act.activation(sm[:, 2, :], sm[:, 1, :], ACT.Exp)
            act.activation(sm[:, 3, 0:SH], head_rows[:, 1, :], ACT.Exp).then_inc(dt_exp, 1)
            act.wait_ge(xs_ps, 1)
            for t in range(TT):
                act.activation(xs_tok[:, t, :], dn[:, t, :], ACT.Copy).then_inc(xs_tok_ready, 1)
            act.wait_ge(cum_ps, 1)
            act.activation(sm[:, 8, :], ps[:, 3, 384:416], ACT.Exp).then_inc(cum_exp, 1)
            for i in range(2 * SG):
                act.wait_ge(dm_ps, i + 1)
                if i >= 2:
                    act.wait_ge(y_ps, i - 1)
                act.activation(decay[i % 2][:, :, :].rearrange("p a b -> p (a b)"), ps[:, i % 2, :],
                               ACT.Exp).then_inc(dm_exp, 1)
            act.wait_ge(y_ready, 2)
            norm("out_ssd")
            dense("out_ssd", 4)

            norm("mla")
            act.wait_ge(k_rope_done, 1)
            for i in range(3):
                split(U0["qup"] + i + 2)
                act.wait_ge(unit_used, U0["qup"] + i + 1)
                act.activation(q_tok[:, 0, :, :].rearrange("p a b -> p (a b)")[:, 512 * i:512 * i + 512],
                               ps[:, 2 * i, :], ACT.Copy).then_inc(q2_act, 1)
            for s in range(4):
                if s % 2 == 0:
                    split(U0["kvup"] + s // 2 + 2)
                if s % 2 == 0:
                    act.wait_ge(kv_ps, s // 2 + 1)
                else:
                    act.wait_ge(unit_used, U0["kvup"] + s // 2 + 1)
                kv = ps[:, (2 * s + 6) % 8, :].rearrange("p (h n) -> p h n", h=4)
                act.activation(k_tok[:, 0, 4 * s:4 * s + 4, 0:NOPE], kv[:, :, 0:NOPE], ACT.Copy)
                act.activation(v_tok[:, 0, 256 * s:256 * s + 256].rearrange("p (h n) -> p h n", h=4), kv[:, :, NOPE:],
                               ACT.Copy).then_inc(kv_act, 1)
            for j in range(0, 16, 2):
                act.wait_ge(mT_ps, j + 1)
                dst = qT2 if j < 8 else kT2
                act.activation(dst[0:QK, 2 * (j % 8):2 * (j % 8) + 2, :], ps[0:QK, j % 8, :].rearrange("p (a b) -> p a b", a=2),
                               ACT.Copy).then_inc(mT_act, 1)
            attention(2, 4)
            norm("out_mla")
            dense("out_mla", 4)

            act.wait_ge(mem_in, 32)
            norm("mk")
            dense("mk", 4)
            act.wait_ge(unit_used, END["mk"])
            act.activation(m_tok[:, 0, :], dn[:, 0, :], ACT.Copy).then_inc(m_act, 1)
            act.wait_ge(m3_ps, 1)
            act.activation(kT3[:, 0:4, :].rearrange("p a b -> p (a b)"), banks(0, 2), ACT.Copy).then_inc(m3_act, 1)
            dense("mv", 4)
            act.wait_ge(unit_used, END["mv"])
            act.activation(v3[:, 0, :], dn[:, 0, :], ACT.Copy).then_inc(m_act, 1)
            norm("mq")
            dense("mq", 4)
            act.wait_ge(unit_used, END["mq"])
            act.activation(m_tok[:, 0, :], dn[:, 0, :], ACT.Copy).then_inc(m_act, 1)
            act.wait_ge(m3_ps, 2)
            act.activation(qT3[:, 0:4, :].rearrange("p a b -> p (a b)"), banks(0, 2), ACT.Copy).then_inc(m3_act, 1)
            attention(6, 2)
            norm("mo")
            dense("mo", 4)
            feed_forward(2, True)
            post("final")

        @block.gpsimd
        def _(pool):
            steps_n = [0]

            def link(ins):
                steps_n[0] += 1
                ins.then_inc(pool_step, 1)
                pool.wait_ge(pool_step, steps_n[0])

            def load_gain(i):
                name = ["ffn1_post", "mix_post", "ffn2_post", "norm_final_w_2"][i]
                src = a[name] if name == "norm_final_w_2" else a[name][0]
                pool.dma_start(gain_row[:, :], src.partition_broadcast(P)).then_inc(gain_in, 16)

            def norm(name):
                n = len(dict(NORMS)[name])
                pool.wait_ge(ssq_done, parts_done(name))
                link(nc.gpsimd.tensor_scalar(rstd[:, :, 0:n], ssq[:, :, 0:n], EPS, None, ALU.add))
                nc.gpsimd.tensor_tensor(rstd[:, :, 0:n], rstd[:, :, 0:n],
                                        neg_half[:, 0:TT * n].rearrange("p (t n) -> p t n", t=TT),
                                        ALU.pow).then_inc(rstd_done, 1)

            def post(name):
                i = POST.index(name)
                pool.wait_ge(post_ssq_done, 2 * i + 2)
                link(nc.gpsimd.tensor_scalar(post_rstd[:, :], post_ssq[:, :], EPS, None, ALU.add))
                nc.gpsimd.tensor_tensor(post_rstd[:, :], post_rstd[:, :], neg_half[:, 0:TT],
                                        ALU.pow).then_inc(post_rstd_done, 1)
                if i < 3:
                    pool.wait_ge(x_ready, 2 * XU.index(name) + 2)
                    load_gain(i + 1)

            nc.gpsimd.memset(neg_half[:, :], -0.5).then_inc(half_ready, 1)
            load_gain(0)
            pool.wait_ge(half_ready, 1)
            norm("f0")
            post("f0")
            norm("win")
            norm("wout")
            post("wout")
            norm("f1")
            post("f1")
            norm("in2")
            pool.wait_ge(adt_ready, 1)
            adt = sm[:, 7, :].rearrange("p (t h) -> p t h", t=TT)

            def step_rows(i):
                if i >= 4:
                    pool.wait_ge(dm_ps, i - 3)
                t, g = i // SG, i % SG
                nc.gpsimd.tensor_tensor(steps[:, 4 * g:4 * g + 4, :], bh(tri, 4), bc(adt[:, t, 4 * g:4 * g + 4], P),
                                        ALU.mult).then_inc(steps_ready, 1)

            for i in range(4):
                step_rows(i)
            pool.wait_ge(xdt_ready, 1)
            pool.wait_ge(cum_exp, 1)
            nc.gpsimd.tensor_tensor(xd_end[:, :].rearrange("p (h n) -> p h n", h=SH),
                                    xdt[:, 0, :].rearrange("p (h n) -> p h n", h=SH),
                                    bc(sm[:, 8, 0:SH], SP_), ALU.mult).then_inc(xd_end_ready, 1)
            for i in range(4, 8):
                step_rows(i)
            for t in range(TT):
                pool.wait_ge(xs_tok_ready, t + 1)
                v = xs_tok[:, t, :].rearrange("p (h n) -> p h n", h=SH)
                nc.gpsimd.tensor_tensor(v, v, bc(head_rows[:, 2, :], SP_), ALU.mult).then_inc(skip_ready, 1)
            norm("out_ssd")
            norm("mla")
            pool.wait_ge(k_rope_done, 1)
            for t in range(TT):
                nc.gpsimd.tensor_copy(k_tok[:, t, :, NOPE:QK], bh(k_rope[:, t, :], MH)).then_inc(k_rope_spread, 1)
            pool.dma_start(qT2[QK:QK + 2, :, :].rearrange("p a b -> p (a b)"), mla_rows[0]).then_inc(mask_rows_in, 16)
            pool.dma_start(kT2[QK:QK + 2, :, :].rearrange("p a b -> p (a b)"), mla_rows[1]).then_inc(mask_rows_in, 16)
            pool.wait_ge(x_ready, 2 * XU.index("out_mla") + 2)
            for t in range(TT):
                pool.dma_start(mem_x[:, t, :], a["mem_2"][0].rearrange("(t p) n -> p t n", p=P)[:, t, :]).then_inc(mem_in, 16)
            norm("mk")
            norm("mq")
            norm("f2")
            fcols = cols[:, FCONV:FCONV + 176].rearrange("p (a n) -> p a n", a=8)

            def taps(c, n):
                nc.gpsimd.tensor_copy(conv_now[:, :, :], fcols[:, :, bass.ds(n, 2)]).then_inc(taps_ready, 1)

            taps(0, 0)
            with pool.Fori(0, NCH - 1) as j:
                pool.wait_ge(tap0, 4 * j + 4)
                taps(j, 2 * j + 2)
            post("final")

        @block.vector
        def _(dve):
            steps_n = [0]

            def link(ins):
                steps_n[0] += 1
                ins.then_inc(dve_step, 1)
                dve.wait_ge(dve_step, steps_n[0])

            TTn = nc.vector.tensor_tensor
            STT = nc.vector.scalar_tensor_tensor

            def split(k, c=0):
                if isinstance(c, int) and k + 3 * c >= UNITS:
                    return
                n = width(k) if isinstance(c, int) else UW
                dve.wait_ge(rounded, 3 * c + (k + 1))
                TTn(w_lo[k % RING][:, 0:n], raw[k % RING][:, 0:n], w_hi[k % RING][:, 0:n].bitcast(F32),
                    ALU.subtract).then_inc(resid, 1)

            def norm(name):
                parts = dict(NORMS)[name]
                if parts:
                    dve.wait_ge(rstd_done, REAL.index(name) + 1)
                    at = 0
                    for i, src in enumerate(mem_parts[name]):
                        for t in range(TT):
                            last = nc.vector.tensor_scalar(xs[:, t, at:at + parts[i]], src[:, t, :], rstd[:, t, i:i + 1],
                                                           None, ALU.mult)
                        at += parts[i]
                    last.then_inc(scaled, 1)
                for k in range(kt_of(name)):
                    dve.wait_ge(xt_hi, kts(name, min(k // 2 * 2 + 2, kt_of(name))))
                    src = ps[:, k // 2, k % 2 * S:k % 2 * S + S]
                    hi = xT_hi[:, k, :].bitcast(F32)
                    if parts:
                        g = col(GAIN[name]) + k
                        STT(out=xT_lo[:, k, :], in0=src, scalar=cols[:, g:g + 1], in1=hi, op0=ALU.mult,
                            op1=ALU.subtract).then_inc(xt_lo, 1)
                    else:
                        TTn(xT_lo[:, k, :], src, hi, ALU.subtract).then_inc(xt_lo, 1)

            def post(name, factor):
                i = POST.index(name)
                dve.wait_ge(post_rstd_done, i + 1)
                dve.wait_ge(gain_in, 16 * (i + 1))
                for t in range(TT):
                    STT(out=xs[:, t, :], in0=dn[:, t, :], scalar=post_rstd[:, t:t + 1], in1=gain_row[:, :],
                        op0=ALU.mult, op1=ALU.mult).then_inc(post_t, 1)
                for t in range(TT):
                    dve.wait_ge(post_t, 2 * i + t + 1)
                    STT(out=X[:, t, :], in0=xs[:, t, :], scalar=factor, in1=X[:, t, :], op0=ALU.mult,
                        op1=ALU.add).then_inc(x_ready, 1)

            def add_to_x(name):
                dve.wait_ge(unit_used, END[name])
                for t in range(TT):
                    TTn(X[:, t, :], dn[:, t, :], X[:, t, :], ALU.add).then_inc(x_ready, 1)

            def chunk(f, conv, k, c, peeled):
                j = c if peeled is None else 0
                fc = f * NCH + (peeled if peeled is not None else 2)
                split(k + 2, j)
                split(k + 3, j)
                if not conv:
                    for t in range(TT):
                        dve.wait_ge(silu_done, 2 * j + (2 * fc + t + 1))
                        TTn(act_s[:, t, :], silu_g[:, t, :], ps[:, t, FC:2 * FC], ALU.mult).then_inc(s_ready, 1)
                if peeled != 0:
                    split(k + 4, j)
                if conv:
                    n = fc - 2 * NCH
                    for tap, first_done in ((1, tap2), (0, tap1)):
                        back = 2 - tap
                        for q in range(4):
                            dve.wait_ge(first_done, 4 * j + (4 * n + (q // 2 * 2 + 1 if tap == 1 else q) + 1))
                            src = ps[:, 2 + q // 2, q % 2 * S:q % 2 * S + S]
                            STT(out=conv_y[:, q, back:S], in0=src[:, 0:S - back],
                                scalar=conv_now[:, 2 * tap + q // 2, q % 2:q % 2 + 1], in1=conv_y[:, q, back:S],
                                op0=ALU.mult, op1=ALU.add).then_inc(tap1 if tap == 1 else tap0, 1)
                    dve.wait_ge(conv_silu, j + (n + 1))
                    TTn(act_s[:, :, :], silu_g[:, :, :], conv_y[:, 2:4, :], ALU.mult).then_inc(conv_s, 1)
                    dve.wait_ge(hT_hi_done, j + (fc + 1))
                    TTn(hT_lo[:, :, :], act_s[:, :, :], hT_hi[:, :, :].bitcast(F32), ALU.subtract).then_inc(hT_lo_done, 1)
                else:
                    dve.wait_ge(hT_hi_done, j + (fc + 1))
                    TTn(hT_lo[:, :, :].rearrange("p a b -> p (a b)"), ps[:, 2, :],
                        hT_hi[:, :, :].rearrange("p a b -> p (a b)").bitcast(F32), ALU.subtract).then_inc(hT_lo_done, 1)

            def feed_forward(f, conv):
                name = f"f{f}"
                u = U0[name]
                norm(name)
                chunk(f, conv, u, 0, 0)
                chunk(f, conv, u + 2, 0, 1)
                with dve.Fori(0, NCH - 3) as j:
                    chunk(f, conv, u + 5, j, None)
                chunk(f, conv, u + 3 * NCH - 4, 0, NCH - 1)
                split(u + 3 * NCH + 1)

            def dense(name, units):
                for i in range(units):
                    split(U0[name] + i + 2)

            def row_max(gi):
                kind, g, nk, hg, dv = GROUPS[gi]
                scale = {"swa": HD ** -0.5, "mla": QK ** -0.5, "mem": MEMD ** -0.5}[kind]
                at, b = 0, gi % 2
                for t in range(TT):
                    n = nk[t] * P
                    dve.wait_ge(sc_ps, 2 * gi + t + 1)
                    link(nc.vector.tensor_reduce(mx[:, t, 0:hg], banks(0, 3)[:, at:at + hg * n].rearrange(
                        "p (h n) -> p h n", h=hg), AX.X, ALU.max))
                    if kind == "swa":
                        sinks = sink_row[:, 4 * g:4 * g + 4]
                        link(STT(out=mx[:, t, 0:hg], in0=mx[:, t, 0:hg], scalar=scale, in1=sinks, op0=ALU.mult, op1=ALU.max))
                        link(nc.vector.tensor_scalar(neg_max[:, b, t, 0:hg], mx[:, t, 0:hg], -1.0, None, ALU.mult))
                        TTn(sink_arg[:, b, t, :], sinks, neg_max[:, b, t, :], ALU.add).then_inc(negm_ready, 1)
                    else:
                        nc.vector.tensor_scalar(neg_max[:, b, t, 0:hg], mx[:, t, 0:hg], -scale, None,
                                                ALU.mult).then_inc(negm_ready, 1)
                    at += hg * n

            def prob_T_out(gi):
                kind, g, nk, hg, dv = GROUPS[gi]
                n = sum(nk) * hg * P
                dve.wait_ge(pT_ps, gi + 1)
                if gi >= 2:
                    dve.wait_ge(o_ps, gi - 1)
                nc.vector.tensor_copy(prob_T(gi)[:, 0:n], banks(3, 3)[:, 0:n]).then_inc(pT_ready, 1)

            def attn_out(gi):
                kind, g, nk, hg, dv = GROUPS[gi]
                dst = {"swa": o1, "mla": o2, "mem": o3}[kind]
                b = gi % 2
                sums = p_sum[:, b, :, 0:hg]
                if kind == "swa":
                    link(TTn(den[:, b, :, 0:hg], sums, sink_exp[:, b, :, 0:hg], ALU.add))
                    sums = den[:, b, :, 0:hg]
                link(nc.vector.reciprocal(rec[:, b, :, 0:hg], sums))
                dve.wait_ge(o_ps, gi + 1)
                for t in range(TT):
                    last = TTn(dst[:, t, g * hg * dv:(g + 1) * hg * dv].rearrange("p (h n) -> p h n", h=hg),
                               ps[:, 6 + t, 0:hg * dv].rearrange("p (h n) -> p h n", h=hg),
                               bc(rec[:, b, t, 0:hg], dv), ALU.mult)
                last.then_inc(o_ready, 1)

            def attention(first, n):
                row_max(first)
                for gi in range(first, first + n):
                    if gi + 1 < first + n:
                        row_max(gi + 1)
                    prob_T_out(gi)
                    attn_out(gi)

            def rope(dst, src, half, sin, cos, tmp):
                (d1, d2), (s1, s2) = dst, src
                TTn(tmp[0], s1, cos, ALU.mult)
                TTn(tmp[1], s2, sin, ALU.mult)
                TTn(tmp[2], s2, cos, ALU.mult)
                link(TTn(tmp[3], s1, sin, ALU.mult))
                TTn(d1, tmp[0], tmp[1], ALU.subtract)
                return TTn(d2, tmp[2], tmp[3], ALU.add)

            dve.wait_ge(small_in, 16 * 7)
            nc.vector.tensor_copy(ident_bf[:, :], ident)
            nc.vector.tensor_copy(mask_bf[:, :], cst[:, C_MASK:C_MASK + 2 * P]).then_inc(consts_bf, 1)
            dve.wait_ge(pos_in, 32)
            link(nc.vector.tensor_copy(pos_f[:, :, :], pos_i[:, :, :]))
            n1 = ROT1 // 2
            for half in range(2):
                for b, (lo, n) in enumerate(((0, n1), (n1, ROT2 // 2))):
                    last = TTn(ang[:, half, :, lo:lo + n], bc(pos_f[:, b, :], n),
                               bh(cst[:, C_FREQ + lo:C_FREQ + lo + n], TT), ALU.mult)
            link(last)
            flat = lambda v: v.rearrange("p a b c -> p (a b c)")
            NA = TT * NFREQ
            for half in range(2):
                last = nc.vector.tensor_scalar(flat(turns[:, :, :, :])[:, half * NA:half * NA + NA],
                                               flat(ang[:, :, :, :])[:, half * NA:half * NA + NA],
                                               float(1 / (2 * np.pi)), 0.25 * half, ALU.mult, ALU.add)
            link(last)
            magic = float(1.5 * 2 ** 23)
            link(nc.vector.tensor_scalar(flat(turns[:, :, :, :]), flat(turns[:, :, :, :]), magic, None, ALU.add))
            link(nc.vector.tensor_scalar(flat(turns[:, :, :, :]), flat(turns[:, :, :, :]), -magic, None, ALU.add))
            c1 = 6.28125
            c2 = float(np.float32(np.round((2 * np.pi - c1) * 2 ** 21) / 2 ** 21))
            for part in (c1, c2, 2 * np.pi - c1 - c2):
                link(STT(out=flat(ang[:, :, :, :]), in0=flat(turns[:, :, :, :]), scalar=-float(part),
                         in1=flat(ang[:, :, :, :]), op0=ALU.mult, op1=ALU.add))
            link(nc.vector.tensor_scalar(flat(ang[:, :, :, :])[:, NA:2 * NA], flat(ang[:, :, :, :])[:, NA:2 * NA],
                                         float(np.pi / 2), None, ALU.add))
            nc.vector.tensor_scalar(flat(ang[:, :, :, :]), flat(ang[:, :, :, :]), 3.1415925, -3.1415925,
                                    ALU.min, ALU.max).then_inc(ang_ready, 1)
            split(0)
            split(1)
            dve.wait_ge(cols_ready, 1)
            feed_forward(0, False)
            post("f0", 0.5)

            norm("win")
            for n in range(3):
                for i in range(2 if n < 2 else 1):
                    split(U0["win"] + 2 * n + i + 2)
                dve.wait_ge(unit_used, min(U0["win"] + 2 * n + 2, END["win"]))
                w = 512 if n < 2 else 256
                nc.vector.tensor_copy(z1[:, 1, 512 * n:512 * n + w], ps[:, 2 * n + 1, 0:w]).then_inc(z1_dve, 1)
            dve.wait_ge(z1_act, 3)
            dve.wait_ge(z1_dve, 3)
            dve.wait_ge(trig_ready, 1)
            qk = z1[:, :, PW:PW + 640].rearrange("p t (h n) -> p t h n", n=HD)
            tmp = [xs[:, 0, 160 * i:160 * i + 160].rearrange("p (h n) -> p h n", h=10) for i in range(4)]
            for t in range(TT):
                h1, h2 = qk[:, t, :, 0:n1], qk[:, t, :, n1:ROT1]
                tm = [v[:, :, t * n1:t * n1 + n1] for v in tmp]
                last = rope((h1, h2), (h1, h2), n1, bh(trig[:, 0, t, 0:n1], 10), bh(trig[:, 1, t, 0:n1], 10), tm)
            last.then_inc(rope1_done, 1)
            link(nc.vector.memset(k_pad[:, :, :, :], 0.0))
            dve.wait_ge(rope1_done, 1)
            for half in range(2):
                for t in range(TT):
                    last = nc.vector.tensor_copy(k_pad[:, t, half::2, half * HD:half * HD + HD],
                                                 z1[:, t, 1024:1152].rearrange("p (g n) -> p g n", g=2))
            last.then_inc(k_pad_done, 1)
            dve.wait_ge(pool_ps, 1)
            for t in range(TT):
                TTn(pool_y[:, t, :], ps[:, t, :], pool_scale[:, :], ALU.mult).then_inc(pool_ready, 1)
            dve.wait_ge(kT1_ps, 1)
            nc.vector.tensor_copy(kT1[:, :, :].rearrange("p a b -> p (a b)"), banks(4, 2)).then_inc(kT1_ready, 1)
            attention(0, 2)
            norm("wout")
            dense("wout", 4)
            post("wout", 1.0)
            feed_forward(1, False)
            post("f1", 0.5)

            norm("in2")
            for n, c in enumerate(IN2_CHUNKS):
                for i in range(1 if c == 7 else 2):
                    split(in2_unit0(n) + i + 2)
                b = n % 2 * 2 + 1
                if n <= 5:
                    dve.wait_ge(unit_used, in2_unit0(n) + (1 if c == 7 else 2))
                if n < 4:
                    if n >= 2:
                        dve.wait_ge(xbT_ps, n - 1)
                    nc.vector.tensor_copy(xbc_in[n % 2][:, 1, :], ps[:, b, :]).then_inc(in2_dve, 1)
                elif c == 6:
                    nc.vector.tensor_copy(tail[:, 1, 0:512], ps[:, b, :]).then_inc(in2_dve, 1)
                elif c == 7:
                    nc.vector.tensor_copy(tail[:, 1, 512:TAILW], ps[:, b, 0:TAILW - 512]).then_inc(in2_dve, 1)
                if 1 <= n <= 4:
                    m = n - 1
                    for back in (1, 2, 3):
                        for q in range(4):
                            ft = 4 * m + q
                            if back == 1:
                                dve.wait_ge(conv_first, 4 * m + q // 2 * 2 + 2)
                            else:
                                dve.wait_ge(conv_tap, 12 * m + 4 * (back - 2) + q + 1)
                            src = ps[:, 4 + m % 2 * 2 + q // 2, q % 2 * S:q % 2 * S + S]
                            w = col("ssd_conv_w_2") + 16 * (3 - back) + ft
                            STT(out=conv_x[:, q, back:S], in0=src[:, 0:S - back], scalar=cols[:, w:w + 1],
                                in1=conv_x[:, q, back:S], op0=ALU.mult, op1=ALU.add).then_inc(conv_tap, 1)
            row = lambda i: sm[:, i, :]
            rowt = lambda i: sm[:, i, :].rearrange("p (t h) -> p t h", t=TT)
            dve.wait_ge(in2_act, 6)
            link(TTn(rowt(0), tail[:, :, 0:SH], bh(head_rows[:, 0, :], TT), ALU.add))
            link(nc.vector.tensor_scalar(row(1), row(0), -1.0, None, ALU.mult))
            TTn(row(1), row(1), row(0), ALU.min).then_inc(dt_arg, 1)
            link(nc.vector.tensor_scalar(row(6), row(0), 0.0, None, ALU.max))
            dve.wait_ge(dt_exp, 1)
            link(nc.vector.tensor_scalar(row(4), row(2), 2.0, None, ALU.add))
            link(nc.vector.reciprocal(row(4), row(4)))
            link(TTn(row(4), row(4), row(2), ALU.mult))
            link(TTn(row(5), row(4), row(4), ALU.mult))
            link(nc.vector.tensor_scalar(row(9), row(5), 1 / 17, None, ALU.mult))
            for d in (15, 13, 11, 9, 7, 5, 3):
                link(STT(out=row(9), in0=row(9), scalar=1 / d, in1=row(5), op0=ALU.add, op1=ALU.mult))
            link(STT(out=row(9), in0=row(9), scalar=1.0, in1=row(4), op0=ALU.add, op1=ALU.mult))
            link(STT(out=row(10), in0=row(9), scalar=2.0, in1=row(6), op0=ALU.mult, op1=ALU.add))
            dtv = rowt(10)
            STT(out=rowt(7), in0=dtv, scalar=-1.0, in1=bh(sm[:, 3, 0:SH], TT), op0=ALU.mult,
                op1=ALU.mult).then_inc(adt_ready, 1)
            for t in range(TT):
                dve.wait_ge(xs_tok_ready, t + 1)
                TTn(xdt[:, t, :].rearrange("p (h n) -> p h n", h=SH), dn[:, t, :].rearrange("p (h n) -> p h n", h=SH),
                    bc(dtv[:, t, :], SP_), ALU.mult).then_inc(xdt_ready, 1)
            for g in range(SG):
                dve.wait_ge(cb_ps, g + 1)
                TTn(cbm[:, g, 0:2 * P].rearrange("p (a b) -> p a b", a=2), ps[:, g, 0:2 * P].rearrange("p (a b) -> p a b", a=2),
                    bh(tri, 2), ALU.mult)
                nc.vector.tensor_copy(cbm[:, g, 2 * P:3 * P], ps[:, g, 2 * P:3 * P]).then_inc(cbm_ready, 1)
            dve.wait_ge(cbm_ready, SG)
            for i in range(2 * SG):
                t, g = i // SG, i % SG
                dve.wait_ge(dm_exp, i + 1)
                TTn(decay[i % 2][:, :, :], decay[i % 2][:, :, :], bh(cbm[:, g, t * P:t * P + P], 4),
                    ALU.mult).then_inc(dm_masked, 1)
            dve.wait_ge(off_ps, 1)
            dve.wait_ge(cum_exp, 1)
            link(TTn(y_ssd[:, 1, :].rearrange("p (h n) -> p h n", h=SH), banks(2, 2).rearrange("p (h n) -> p h n", h=SH),
                     bc(sm[:, 8, SH:2 * SH], SP_), ALU.mult))
            dve.wait_ge(y_ps, 2 * SG)
            dve.wait_ge(skip_ready, 2)
            TTn(y_ssd[:, 0, :], dn[:, 0, :], xs_tok[:, 0, :], ALU.add)
            link(TTn(y_ssd[:, 1, :], dn[:, 1, :], y_ssd[:, 1, :], ALU.add))
            link(TTn(y_ssd[:, 1, :], y_ssd[:, 1, :], xs_tok[:, 1, :], ALU.add))
            dve.wait_ge(in2_act, 8)
            for t in range(TT):
                TTn(y_ssd[:, t, :], y_ssd[:, t, :], zg[:, t, :], ALU.mult).then_inc(y_ready, 1)
            norm("out_ssd")
            dense("out_ssd", 4)
            add_to_x("out_ssd")

            norm("mla")
            n2 = ROT2 // 2
            src = [tail[:, :, T_KR:T_KR + n2], tail[:, :, T_KR + n2:T_KR + ROPE]]
            tmp = [xs[:, 1, 640 + 32 * i:672 + 32 * i].rearrange("p (t n) -> p t n", t=TT) for i in range(4)]
            sin2, cos2 = trig[:, 0, :, n1:NFREQ], trig[:, 1, :, n1:NFREQ]
            rope((k_rope[:, :, 0:n2], k_rope[:, :, n2:ROPE]), src, n2, sin2, cos2, tmp).then_inc(k_rope_done, 1)
            dve.wait_ge(k_rope_done, 1)
            for i in range(3):
                split(U0["qup"] + i + 2)
                dve.wait_ge(unit_used, U0["qup"] + i + 1)
                nc.vector.tensor_copy(q_tok[:, 1, :, :].rearrange("p a b -> p (a b)")[:, 512 * i:512 * i + 512],
                                      ps[:, 2 * i + 1, :]).then_inc(q2_dve, 1)
            for s in range(4):
                if s % 2 == 0:
                    split(U0["kvup"] + s // 2 + 2)
                if s % 2 == 0:
                    dve.wait_ge(kv_ps, s // 2 + 1)
                else:
                    dve.wait_ge(unit_used, U0["kvup"] + s // 2 + 1)
                kv = ps[:, (2 * s + 7) % 8, :].rearrange("p (h n) -> p h n", h=4)
                nc.vector.tensor_copy(k_tok[:, 1, 4 * s:4 * s + 4, 0:NOPE], kv[:, :, 0:NOPE])
                nc.vector.tensor_copy(v_tok[:, 1, 256 * s:256 * s + 256].rearrange("p (h n) -> p h n", h=4),
                                      kv[:, :, NOPE:]).then_inc(kv_dve, 1)
            dve.wait_ge(q2_act, 3)
            dve.wait_ge(q2_dve, 3)
            for t in range(TT):
                tmp = [xs[:, :, :].rearrange("p t n -> p (t n)")[:, 512 * i + 256 * t:512 * i + 256 * t + 256]
                       .rearrange("p (h n) -> p h n", h=MH) for i in range(4)]
                h1, h2 = q_tok[:, t, :, NOPE:NOPE + n2], q_tok[:, t, :, NOPE + n2:QK]
                last = rope((h1, h2), (h1, h2), n2, bh(sin2[:, t, :], MH), bh(cos2[:, t, :], MH), tmp)
            last.then_inc(rope2_done, 1)
            for j in range(1, 16, 2):
                dve.wait_ge(mT_ps, j + 1)
                dst = qT2 if j < 8 else kT2
                nc.vector.tensor_copy(dst[0:QK, 2 * (j % 8):2 * (j % 8) + 2, :],
                                      ps[0:QK, j % 8, :].rearrange("p (a b) -> p a b", a=2)).then_inc(mT_dve, 1)
            attention(2, 4)
            norm("out_mla")
            dense("out_mla", 4)
            add_to_x("out_mla")

            norm("mk")
            dense("mk", 4)
            dve.wait_ge(unit_used, END["mk"])
            nc.vector.tensor_copy(m_tok[:, 1, :], dn[:, 1, :]).then_inc(m_dve, 1)
            dve.wait_ge(m3_ps, 1)
            nc.vector.tensor_copy(kT3[:, 4:8, :].rearrange("p a b -> p (a b)"), banks(2, 2)).then_inc(m3_dve, 1)
            dense("mv", 4)
            dve.wait_ge(unit_used, END["mv"])
            nc.vector.tensor_copy(v3[:, 1, :], dn[:, 1, :]).then_inc(m_dve, 1)
            norm("mq")
            dense("mq", 4)
            dve.wait_ge(unit_used, END["mq"])
            nc.vector.tensor_copy(m_tok[:, 1, :], dn[:, 1, :]).then_inc(m_dve, 1)
            dve.wait_ge(m3_ps, 2)
            nc.vector.tensor_copy(qT3[:, 4:8, :].rearrange("p a b -> p (a b)"), banks(2, 2)).then_inc(m3_dve, 1)
            attention(6, 2)
            norm("mo")
            dense("mo", 4)
            add_to_x("mo")
            feed_forward(2, True)
            add_to_x("f2")
            dve.wait_ge(post_rstd_done, 4)
            dve.wait_ge(gain_in, 64)
            for t in range(TT):
                STT(out=xs[:, t, :], in0=X[:, t, :], scalar=post_rstd[:, t:t + 1], in1=gain_row[:, :],
                    op0=ALU.mult, op1=ALU.mult).then_inc(x_ready, 1)

        @block.tensor
        def _(pe):
            def product(out_, lhs, rhs, first, last):
                (lh, ll), (rh, rl) = lhs, rhs
                pe.matmul(out_, lh, rh, start=first, stop=False)
                pe.matmul(out_, lh, rl, start=False, stop=False)
                return pe.matmul(out_, ll, rh, start=False, stop=last)

            def xT(k, t):
                return xT_hi[:, k, t * P:t * P + P], xT_lo[:, k, t * P:t * P + P]

            def wt(k, at, n):
                return w_hi[k % RING][:, at:at + n], w_lo[k % RING][:, at:at + n]

            def norm(name):
                if dict(NORMS)[name]:
                    pe.wait_ge(scaled, REAL.index(name) + 1)
                    src = xs
                else:
                    src = {"out_mla": o2, "mo": o3}[name]
                for k in range(kt_of(name)):
                    for t in range(TT):
                        last = pe.transpose(ps[:, k // 2, k % 2 * S + t * P:k % 2 * S + t * P + P],
                                            src[:, t, k * P:k * P + P], ident)
                    last.then_inc(xt_ps, 1)
                pe.wait_ge(xt_lo, kts(name, kt_of(name)))

            def by_rows(name, i):
                k = U0[name] + i
                pe.wait_ge(resid, k + 1)
                for r in range(2):
                    for t in range(TT):
                        for h in range(2):
                            last = product(dn[:, t, 512 * h:512 * h + 512], xT(2 * i + r, t),
                                           wt(k, 1024 * r + 512 * h, 512), i == 0 and r == 0, i == 3 and r == 1)
                last.then_inc(unit_used, 1)

            def to_1024(name):
                for i in range(4):
                    by_rows(name, i)

            def chunk(k, b, n=512):
                for half in range(2):
                    pe.wait_ge(resid, k + half + 1)
                    for t in range(TT):
                        for r in range(4):
                            last = product(ps[:, b + t, 0:n], xT(4 * half + r, t), wt(k + half, n * r, n),
                                           half == 0 and r == 0, half == 1 and r == 3)
                    last.then_inc(unit_used, 1)

            def narrow(k, b, nk, at, n, stride, end=True):
                pe.wait_ge(resid, k + 1)
                for t in range(TT):
                    for r in range(nk):
                        last = product(ps[:, (b + t) % 8, 0:n], xT(r, t), wt(k, stride * r + at, n), r == 0, r == nk - 1)
                return last

            def gate_up(k, j):
                for half in range(2):
                    pe.wait_ge(resid, 3 * j + (k + half + 1))
                    for t in range(TT):
                        for r in range(4):
                            last = product(ps[:, t, :], xT(4 * half + r, t), wt(k + half, 512 * r, 512),
                                           half == 0 and r == 0, half == 1 and r == 3)
                        if half == 1 and t == 0:
                            last.then_inc(gu_ps, 1)
                    last.then_inc(unit_used, 1)

            def down(k, j, n_hT, first, final):
                pe.wait_ge(hT_lo_done, j + n_hT)
                pe.wait_ge(resid, 3 * j + (k + 1))
                for r in range(2):
                    for t in range(TT):
                        for h in range(2):
                            last = product(dn[:, t, 512 * h:512 * h + 512],
                                           (hT_hi[:, r, t * P:t * P + P], hT_lo[:, r, t * P:t * P + P]),
                                           wt(k, 1024 * r + 512 * h, 512), first and r == 0, final and r == 1)
                last.then_inc(unit_used, 1)

            def turn(f, conv, j, c):
                if conv:
                    for t in range(TT):
                        pe.wait_ge(u_ready, 2 * j + (2 * c + t + 1))
                        for q in range(4):
                            last = pe.transpose(ps[:, 2 + q // 2, q % 2 * S + t * P:q % 2 * S + t * P + P],
                                                act_in[:, t, q * P:q * P + P], ident)
                    last.then_inc(uT_ps, 1)
                else:
                    for t in range(TT):
                        pe.wait_ge(s_ready, 2 * j + (2 * (f * NCH + c) + t + 1))
                        for q in range(2):
                            last = pe.transpose(ps[:, 2, q * S + t * P:q * S + t * P + P],
                                                act_s[:, t, q * P:q * P + P], ident)
                    last.then_inc(hT_ps, 1)

            def feed_forward(f, conv):
                name = f"f{f}"
                u = U0[name]
                norm(name)
                gate_up(u, 0)
                turn(f, conv, 0, 0)
                gate_up(u + 2, 0)
                down(u + 4, 0, f * NCH + 1, True, False)
                turn(f, conv, 0, 1)
                with pe.Fori(0, NCH - 3) as j:
                    gate_up(u + 5, j)
                    down(u + 7, j, f * NCH + 2, False, False)
                    turn(f, conv, j, 2)
                gate_up(u + 3 * NCH - 4, 0)
                down(u + 3 * NCH - 2, 0, f * NCH + NCH - 1, False, False)
                turn(f, conv, 0, NCH - 1)
                down(u + 3 * NCH - 1, 0, f * NCH + NCH, False, True)

            def scores(gi):
                kind, g, nk, hg, dv = GROUPS[gi]
                if gi and GROUPS[gi - 1][0] == kind:
                    pe.wait_ge(p_ready, 2 * gi)
                at = 0
                for t in range(TT):
                    n = nk[t] * P
                    keys = slice(0, n)
                    if kind == "swa":
                        per = 512 // n
                        for b in range(hg // per):
                            out_ = banks(0, 3)[:, at + 512 * b:at + 512 * b + 512].rearrange("p (h n) -> p h n", h=per)
                            pe.matmul(out_, ident_bf[:, :], bh(mask_bf[:, 2 * P - n:2 * P], per), start=True, stop=True)
                            for h in range(per * b, per * b + per):
                                head = 4 * g + h
                                last = pe.matmul(banks(0, 3)[:, at + h * n:at + h * n + n],
                                                 qT1[:, head // 2, t * P:t * P + P], kT1[:, 2 * g + head % 2, keys], start=False, stop=True,
                                                 skip_group_check=True)
                    else:
                        for h in range(hg):
                            head = hg * g + h
                            out_ = banks(0, 3)[:, at + h * n:at + h * n + n]
                            if kind == "mla":
                                last = pe.matmul(out_, qT2[0:QK + 2, head, t * P:t * P + P], kT2[0:QK + 2, head, keys],
                                                 start=True, stop=True)
                            else:
                                for d in range(2):
                                    last = pe.matmul(out_, qT3[:, 2 * head + d, t * P:t * P + P],
                                                     kT3[:, 2 * head + d, keys], start=(d == 0), stop=(d == 1))
                    last.then_inc(sc_ps, 1)
                    at += hg * n

            def turn_probs(gi):
                kind, g, nk, hg, dv = GROUPS[gi]
                pe.wait_ge(p_ready, 2 * gi + 2)
                if gi and GROUPS[gi - 1][0] == kind:
                    pe.wait_ge(pT_ready, gi)
                for i in range(sum(nk) * hg):
                    last = pe.transpose(banks(3, 3)[:, i * P:i * P + P], prob(gi)[:, i * P:i * P + P], ident)
                last.then_inc(pT_ps, 1)

            def weighted(gi):
                kind, g, nk, hg, dv = GROUPS[gi]
                pe.wait_ge(pT_ready, gi + 1)
                if gi and GROUPS[gi - 1][0] == kind:
                    pe.wait_ge(o_ready, gi)
                i = 0
                for t in range(TT):
                    for h in range(hg):
                        for kt in range(nk[t]):
                            if kind == "swa":
                                v = z1[:, kt, 1152 + HD * g:1152 + HD * g + HD]
                            elif kind == "mla":
                                v = v_tok[:, kt, (4 * g + h) * MV:(4 * g + h + 1) * MV]
                            else:
                                v = v3[:, kt, (hg * g + h) * MEMD:(hg * g + h + 1) * MEMD]
                            last = pe.matmul(ps[:, 6 + t, h * dv:h * dv + dv], prob_T(gi)[:, i * P:i * P + P], v,
                                             start=(kt == 0), stop=(kt == nk[t] - 1))
                            i += 1
                last.then_inc(o_ps, 1)

            def attention(first, n):
                scores(first)
                for gi in range(first, first + n):
                    if gi + 1 < first + n:
                        scores(gi + 1)
                    turn_probs(gi)
                    weighted(gi)

            pe.wait_ge(small_in, 16 * 7)
            pe.wait_ge(rows_in, 16 * (len(ROWS) + 3))
            for i, n in enumerate(ROW_TILES):
                last = pe.transpose(ps[:, 7, COL_AT[i]:COL_AT[i] + n], rows[0:n, i, :], ident_n(n))
            last.then_inc(cols_ps, 1)
            feed_forward(0, False)

            norm("win")
            u = U0["win"]
            chunk(u, 0)
            chunk(u + 2, 2)
            pe.wait_ge(x_ready, 2)
            narrow(u + 4, 4, 8, 0, 256, 256).then_inc(unit_used, 1)
            pe.wait_ge(z1_act, 1)
            pe.wait_ge(z1_dve, 1)
            for g in range(4):
                at = C_BAND + 384 * g
                out_ = ps[:, 6 + g // 2, g % 2 * S:g % 2 * S + S]
                pe.matmul(out_, z1[:, 0, g * P:g * P + P], cst[:, at:at + S], start=True, stop=True)
                last = pe.matmul(out_[:, P:S], z1[:, 1, g * P:g * P + P], cst[:, at + S:at + S + P], start=False, stop=True,
                                 skip_group_check=True)
            last.then_inc(dT_ps, 1)
            pe.wait_ge(dT_ready, 1)
            for t in range(TT):
                for g in range(4):
                    last = pe.matmul(ps[:, t, g * P:g * P + P], dT[:, g, t * P:t * P + P], w_pool_sb[:, g, :],
                                     start=True, stop=True)
            last.then_inc(pool_ps, 1)
            pe.wait_ge(rope1_done, 1)
            for q in range(4):
                for t in range(TT):
                    last = pe.transpose(ps[:, 2 + q // 2, q % 2 * S + t * P:q % 2 * S + t * P + P],
                                        z1[:, t, PW + q * P:PW + q * P + P], ident)
            last.then_inc(qT1_ps, 1)
            pe.wait_ge(k_pad_done, 1)
            for g in range(4):
                for t in range(TT):
                    last = pe.transpose(ps[:, 4 + g // 2, g % 2 * S + t * P:g % 2 * S + t * P + P], k_pad[:, t, g, :], ident)
            last.then_inc(kT1_ps, 1)
            pe.wait_ge(qT1_ready, 1)
            pe.wait_ge(kT1_ready, 1)
            pe.wait_ge(pool_ready, 2)
            attention(0, 2)
            pe.wait_ge(o_ready, 2)
            norm("wout")
            to_1024("wout")
            feed_forward(1, False)

            norm("in2")
            for n, c in enumerate(IN2_CHUNKS):
                if n >= 2:
                    pe.wait_ge(in2_act, n - 1)
                    pe.wait_ge(in2_dve, n - 1)
                if c == 7:
                    narrow(in2_unit0(n), n % 2 * 2, 8, 0, IN2 - 3584, IN2 - 3584).then_inc(unit_used, 1)
                else:
                    chunk(in2_unit0(n), n % 2 * 2)
                m = n - 1
                if 0 <= m < 4:
                    pe.wait_ge(in2_act, m + 1)
                    pe.wait_ge(in2_dve, m + 1)
                    if m < 2:
                        pe.wait_ge(x_ready, 6)
                    else:
                        pe.wait_ge(conv_tap, 12 * (m - 1))
                    for q in range(4):
                        for t in range(TT):
                            last = pe.transpose(ps[:, 4 + m % 2 * 2 + q // 2, q % 2 * S + t * P:q % 2 * S + t * P + P],
                                                xbc_in[m % 2][:, t, q * P:q * P + P], ident)
                    last.then_inc(xbT_ps, 1)
            pe.wait_ge(xbc_ready, 4)
            for t in range(TT):
                for ft in range(8):
                    last = pe.transpose(dn[:, t, ft * P:ft * P + P], xbcT[:, ft, t * P:t * P + P], ident)
            last.then_inc(xs_ps, 1)
            pe.wait_ge(in2_act, 8)
            for g in range(SG):
                for i, (s_, l_) in enumerate(((0, 0), (1, 1), (0, 1))):
                    last = pe.matmul(ps[:, g, i * P:i * P + P], xbcT[:, 8 + g, s_ * P:s_ * P + P],
                                     xbcT[:, 12 + g, l_ * P:l_ * P + P], start=True, stop=True)
                last.then_inc(cb_ps, 1)
            pe.wait_ge(adt_ready, 1)
            pe.wait_ge(cbm_ready, 4)
            pe.matmul(ps[:, 3, 384:400], later, sm[:, 7, 0:SH], start=True, stop=True)
            pe.matmul(ps[:, 3, 400:416], tri, sm[:, 7, SH:2 * SH], start=True, stop=True).then_inc(cum_ps, 1)

            def decay_sums(i):
                t, g = i // SG, i % SG
                pe.wait_ge(steps_ready, i + 1)
                if i < 2:
                    pe.wait_ge(cbm_ready, 4)
                else:
                    pe.wait_ge(dm_exp, i - 1)
                pe.matmul(ps[:, i % 2, :], later, steps[:, 4 * g:4 * g + 4, :].rearrange("p a b -> p (a b)"),
                          start=True, stop=True).then_inc(dm_ps, 1)

            decay_sums(0)
            pe.wait_ge(xs_tok_ready, 2)
            pe.wait_ge(xdt_ready, 2)
            for i in range(2 * SG):
                t, g = i // SG, i % SG
                if i + 1 < 2 * SG:
                    decay_sums(i + 1)
                pe.wait_ge(dm_masked, i + 1)
                for h in range(4):
                    at = (4 * g + h) * SP_
                    last = pe.matmul(dn[:, t, at:at + SP_], decay[i % 2][:, h, :], xdt[:, t, at:at + SP_], start=True, stop=True)
                last.then_inc(y_ps, 1)
                if i == 3:
                    pe.wait_ge(xd_end_ready, 1)
                    pe.wait_ge(cum_exp, 1)
                    for g_ in range(SG):
                        last = pe.matmul(banks(2, 2)[:, g_ * 256:g_ * 256 + 256], cbm[:, g_, 2 * P:3 * P],
                                         xd_end[:, g_ * 256:g_ * 256 + 256], start=True, stop=True)
                    last.then_inc(off_ps, 1)
            norm("out_ssd")
            to_1024("out_ssd")

            norm("mla")
            pe.wait_ge(x_ready, 2 * XU.index("out_ssd") + 2)
            for i in range(3):
                narrow(U0["qup"] + i, 2 * i, 3, 0, 512, 512).then_inc(unit_used, 1)
            for s_ in range(4):
                k = U0["kvup"] + s_ // 2
                pe.wait_ge(resid, k + 1)
                if s_:
                    pe.wait_ge(q2_act, s_)
                    pe.wait_ge(q2_dve, s_)
                for t in range(TT):
                    for r in range(2):
                        last = product(ps[:, (2 * s_ + 6 + t) % 8, :], xT(3 + r, t), wt(k, 1024 * r + 512 * (s_ % 2), 512),
                                       r == 0, r == 1)
                last.then_inc(unit_used if s_ % 2 else kv_ps, 1)
            pe.wait_ge(rope2_done, 1)
            pe.wait_ge(kv_act, 4)
            pe.wait_ge(kv_dve, 4)
            pe.wait_ge(k_rope_spread, 2)
            for j in range(16):
                if j >= 8:
                    pe.wait_ge(mT_act if j % 2 == 0 else mT_dve, (j - 8) // 2 + 1)
                src = q_tok if j < 8 else k_tok
                for h in range(2):
                    for t in range(TT):
                        last = pe.transpose(ps[0:QK, j % 8, h * S + t * P:h * S + t * P + P],
                                            src[:, t, 2 * (j % 8) + h, :], ident)
                last.then_inc(mT_ps, 1)
            pe.wait_ge(mT_act, 8)
            pe.wait_ge(mT_dve, 8)
            pe.wait_ge(mask_rows_in, 32)
            attention(2, 4)
            pe.wait_ge(o_ready, 6)
            norm("out_mla")
            to_1024("out_mla")

            def turn_m():
                for k in range(KT):
                    for t in range(TT):
                        last = pe.transpose(ps[:, k // 2, k % 2 * S + t * P:k % 2 * S + t * P + P],
                                            m_tok[:, t, k * P:k * P + P], ident)
                last.then_inc(m3_ps, 1)

            norm("mk")
            pe.wait_ge(x_ready, 2 * XU.index("out_mla") + 2)
            to_1024("mk")
            pe.wait_ge(m_act, 1)
            pe.wait_ge(m_dve, 1)
            turn_m()
            to_1024("mv")
            pe.wait_ge(m3_act, 1)
            pe.wait_ge(m3_dve, 1)
            norm("mq")
            pe.wait_ge(m_act, 2)
            pe.wait_ge(m_dve, 2)
            to_1024("mq")
            pe.wait_ge(m_act, 3)
            pe.wait_ge(m_dve, 3)
            turn_m()
            pe.wait_ge(m3_act, 2)
            pe.wait_ge(m3_dve, 2)
            attention(6, 2)
            pe.wait_ge(o_ready, 8)
            norm("mo")
            to_1024("mo")
            feed_forward(2, True)


_NAMES = ["x", "positions", "ffn1_pre", "ffn1_w_gu", "ffn1_w_down", "ffn1_post", "mix_pre", "w_in", "w_pool",
          "pool_scale", "sinks", "g_pool", "g_attn", "w_out", "mix_post", "ffn2_pre", "ffn2_w_gu", "ffn2_w_down",
          "ffn2_post", "mem_2", "positions_2", "norm_mix_w_2", "w_in_2", "ssd_conv_w_2", "ssd_conv_b_2",
          "ssd_dt_bias_2", "ssd_a_log_2", "ssd_d_2", "ssd_norm_w_2", "mla_q_norm_w_2", "mla_w_q_up_2",
          "mla_kv_norm_w_2", "mla_w_kv_up_2", "w_out_2", "norm_memx_w_2", "norm_mem_w_2", "w_mem_q_2", "w_mem_k_2",
          "w_mem_v_2", "w_mem_o_2", "norm_ffn_w_2", "w_ffn_up_2", "ffn_conv_w_2", "ffn_conv_b_2", "w_ffn_down_2",
          "norm_final_w_2"]


def kernel(**inputs):
    import concourse.bacc as bacc
    from concourse.bass_utils import run_bass_kernel_spmd

    nc = bacc.Bacc("TRN2", target_bir_lowering=False, num_devices=1)
    arrays, aps = {}, {}
    for name in _NAMES:
        v = np.ascontiguousarray(inputs[name])
        arrays[f"in_{name}"] = v
        aps[name] = nc.dram_tensor(f"in_{name}", v.shape, mybir.dt.from_np(v.dtype), kind="ExternalInput").ap()
    fixed = []
    for name, v in zip(("shape_constants", "mla_mask_rows"), constants()):
        arrays[name] = v
        fixed.append(nc.dram_tensor(name, v.shape, F32, kind="ExternalInput").ap())
    out = nc.dram_tensor("out", (1, S, D), F32, kind="ExternalOutput").ap()
    two_blocks(nc, aps, fixed[0], fixed[1], out)
    r = run_bass_kernel_spmd(nc, [arrays], core_ids=[0])
    return r.results[0]["out"]
```
